# Optimizing a Trainium2 kernel written in Bass

```python
import jax, jax.numpy as jnp
from jax import lax
import numpy as np

D_MODEL = 1024
BATCH = 1
SEQ = 256
DEPTH = 2

N_A = (DEPTH + 1) // 2
N_B = DEPTH // 2

D_RNN = D_MODEL
N_RNN_BLOCKS = 8
RNN_BLOCK = D_RNN // N_RNN_BLOCKS
CONV_WIDTH = 4
LRU_C = 8.0

N_HEADS = 16
N_KV_HEADS = 4
HEAD_DIM = 64
GROUP = N_HEADS // N_KV_HEADS
Q_DIM = N_HEADS * HEAD_DIM
KV_DIM = N_KV_HEADS * HEAD_DIM
WINDOW = 128
ATTN_BLOCK = 128
ROPE_THETA = 500000.0
ROT_DIM = HEAD_DIM // 4

D_FF = 3584
N_EXPERTS = 8
TOP_K = 2

EPS = 1e-6
NEG_INF = -1e30

kernel_name = "hybrid_rglru_swa_sink_moe_trunk"

def rmsnorm(t, g):
    tf = t.astype(jnp.float32)
    tf = tf * lax.rsqrt(jnp.mean(tf * tf, axis=-1, keepdims=True) + EPS)
    return (tf * g.astype(jnp.float32)).astype(t.dtype)

def rope_tables(positions):
    inv_freq = ROPE_THETA ** (-jnp.arange(0, ROT_DIM, 2, dtype=jnp.float32) / ROT_DIM)
    ang = positions.astype(jnp.float32)[..., None] * inv_freq
    return jnp.cos(ang)[:, :, None, :], jnp.sin(ang)[:, :, None, :]

def apply_partial_rope(t, cos, sin):
    rot, keep = t[..., :ROT_DIM].astype(jnp.float32), t[..., ROT_DIM:]
    t1, t2 = rot[..., :ROT_DIM // 2], rot[..., ROT_DIM // 2:]
    rot = jnp.concatenate([t1 * cos - t2 * sin, t2 * cos + t1 * sin], axis=-1).astype(t.dtype)
    return jnp.concatenate([rot, keep], axis=-1)

def rglru_mixer(h, w_in, conv_w, conv_b, w_a, b_a, w_x, b_x, lam, w_out):
    B, S, _ = h.shape
    proj = h @ w_in
    y_branch, x_branch = jnp.split(proj, 2, axis=-1)
    y_branch = jax.nn.gelu(y_branch, approximate=True)
    xp = jnp.pad(x_branch, ((0, 0), (CONV_WIDTH - 1, 0), (0, 0)))
    xc = conv_b + sum(xp[:, k:k + S] * conv_w[k] for k in range(CONV_WIDTH))
    xb = xc.reshape(B, S, N_RNN_BLOCKS, RNN_BLOCK)
    r = jax.nn.sigmoid(jnp.einsum('bsnc,ncd->bsnd', xb, w_a).reshape(B, S, D_RNN) + b_a)
    i = jax.nn.sigmoid(jnp.einsum('bsnc,ncd->bsnd', xb, w_x).reshape(B, S, D_RNN) + b_x)
    log_a = -LRU_C * r.astype(jnp.float32) * jax.nn.softplus(-lam.astype(jnp.float32))
    a = jnp.exp(log_a)
    gated_x = jnp.sqrt(-jnp.expm1(2.0 * log_a)) * (i * xc).astype(jnp.float32)

    def combine(left, right):
        a1, b1 = left
        a2, b2 = right
        return a1 * a2, a2 * b1 + b2

    _, hs = lax.associative_scan(combine, (a, gated_x), axis=1)
    return (hs.astype(h.dtype) * y_branch) @ w_out

def swa_sink_mixer(h, cos, sin, w_qkv, b_qkv, sinks, w_o, b_o):
    B, S, _ = h.shape
    nb = S // ATTN_BLOCK
    qkv = h @ w_qkv + b_qkv
    q, k, v = jnp.split(qkv, [Q_DIM, Q_DIM + KV_DIM], axis=-1)
    q = apply_partial_rope(q.reshape(B, S, N_HEADS, HEAD_DIM), cos, sin)
    k = apply_partial_rope(k.reshape(B, S, N_KV_HEADS, HEAD_DIM), cos, sin)
    v = v.reshape(B, S, N_KV_HEADS, HEAD_DIM)
    qb = q.reshape(B, nb, ATTN_BLOCK, N_KV_HEADS, GROUP, HEAD_DIM)
    kb = k.reshape(B, nb, ATTN_BLOCK, N_KV_HEADS, HEAD_DIM)
    vb = v.reshape(B, nb, ATTN_BLOCK, N_KV_HEADS, HEAD_DIM)

    def with_prev(t):
        prev = jnp.pad(t, ((0, 0), (1, 0), (0, 0), (0, 0), (0, 0)))[:, :-1]
        return jnp.concatenate([prev, t], axis=2)

    kc, vc = with_prev(kb), with_prev(vb)
    scores = jnp.einsum('bnqkgd,bnjkd->bnkgqj', qb, kc).astype(jnp.float32) * (HEAD_DIM ** -0.5)
    blk = jnp.arange(nb)[:, None, None]
    qpos = blk * ATTN_BLOCK + jnp.arange(ATTN_BLOCK)[None, :, None]
    kpos = (blk - 1) * ATTN_BLOCK + jnp.arange(2 * ATTN_BLOCK)[None, None, :]
    allowed = (kpos <= qpos) & (kpos > qpos - WINDOW) & (kpos >= 0)
    scores = jnp.where(allowed[None, :, None, None], scores, NEG_INF)
    sink = jnp.broadcast_to(sinks.astype(jnp.float32).reshape(1, 1, N_KV_HEADS, GROUP, 1, 1),
                            scores.shape[:-1] + (1,))
    probs = jax.nn.softmax(jnp.concatenate([scores, sink], axis=-1), axis=-1)[..., :-1]
    o = jnp.einsum('bnkgqj,bnjkd->bnqkgd', probs.astype(vc.dtype), vc).reshape(B, S, Q_DIM)
    return o @ w_o + b_o

def swiglu(h, w_gate, w_up, w_down):
    return (jax.nn.silu(h @ w_gate) * (h @ w_up)) @ w_down

def moe_swiglu(h, w_router, w_gate, w_up, w_down):
    logits = (h @ w_router).astype(jnp.float32)
    top_vals, top_idx = lax.top_k(logits, TOP_K)
    gates = jax.nn.softmax(top_vals, axis=-1)
    comb = jnp.sum(jax.nn.one_hot(top_idx, N_EXPERTS, dtype=jnp.float32) * gates[..., None], axis=-2)
    out = jnp.zeros_like(h)
    for e in range(N_EXPERTS):
        out = out + comb[..., e:e + 1].astype(h.dtype) * swiglu(h, w_gate[e], w_up[e], w_down[e])
    return out

def _normal(k, shape, scale):
    return jax.random.normal(k, shape, jnp.float32) * scale

def setup_inputs(seed: int = 0) -> dict:
    key = jax.random.key(seed)
    ks = jax.random.split(key, 32)
    u = jax.random.uniform(ks[9], (N_A, D_RNN), jnp.float32, 0.9, 0.999)
    s = u ** (1.0 / LRU_C)
    return {
        "x": _normal(ks[0], (BATCH, SEQ, D_MODEL), 1.0),
        "positions": jnp.broadcast_to(jnp.arange(SEQ, dtype=jnp.int32), (BATCH, SEQ)),
        "norm_mix": 1.0 + _normal(ks[1], (DEPTH, D_MODEL), 0.02),
        "norm_ffn": 1.0 + _normal(ks[2], (DEPTH, D_MODEL), 0.02),
        "norm_final": 1.0 + _normal(ks[3], (D_MODEL,), 0.02),
        "lru_w_in": _normal(ks[4], (N_A, D_MODEL, 2 * D_RNN), D_MODEL ** -0.5),
        "lru_conv_w": _normal(ks[5], (N_A, CONV_WIDTH, D_RNN), CONV_WIDTH ** -0.5),
        "lru_conv_b": _normal(ks[6], (N_A, D_RNN), 0.02),
        "lru_w_a": _normal(ks[7], (N_A, N_RNN_BLOCKS, RNN_BLOCK, RNN_BLOCK), RNN_BLOCK ** -0.5),
        "lru_b_a": _normal(ks[8], (N_A, D_RNN), 0.02),
        "lru_w_x": _normal(ks[10], (N_A, N_RNN_BLOCKS, RNN_BLOCK, RNN_BLOCK), RNN_BLOCK ** -0.5),
        "lru_b_x": _normal(ks[11], (N_A, D_RNN), 0.02),
        "lru_lambda": jnp.log(s) - jnp.log1p(-s),
        "lru_w_out": _normal(ks[12], (N_A, D_RNN, D_MODEL), D_RNN ** -0.5),
        "attn_w_qkv": _normal(ks[13], (N_B, D_MODEL, Q_DIM + 2 * KV_DIM), D_MODEL ** -0.5),
        "attn_b_qkv": _normal(ks[14], (N_B, Q_DIM + 2 * KV_DIM), 0.02),
        "attn_sinks": _normal(ks[15], (N_B, N_HEADS), 1.0),
        "attn_w_o": _normal(ks[16], (N_B, Q_DIM, D_MODEL), Q_DIM ** -0.5),
        "attn_b_o": _normal(ks[17], (N_B, D_MODEL), 0.02),
        "ffn_w_gate": _normal(ks[18], (N_A, D_MODEL, D_FF), D_MODEL ** -0.5),
        "ffn_w_up": _normal(ks[19], (N_A, D_MODEL, D_FF), D_MODEL ** -0.5),
        "ffn_w_down": _normal(ks[20], (N_A, D_FF, D_MODEL), D_FF ** -0.5),
        "moe_w_router": _normal(ks[21], (N_B, D_MODEL, N_EXPERTS), D_MODEL ** -0.5),
        "moe_w_gate": _normal(ks[22], (N_B, N_EXPERTS, D_MODEL, D_FF), D_MODEL ** -0.5),
        "moe_w_up": _normal(ks[23], (N_B, N_EXPERTS, D_MODEL, D_FF), D_MODEL ** -0.5),
        "moe_w_down": _normal(ks[24], (N_B, N_EXPERTS, D_FF, D_MODEL), D_FF ** -0.5),
    }

def reference(x, positions, norm_mix, norm_ffn, norm_final,
              lru_w_in, lru_conv_w, lru_conv_b, lru_w_a, lru_b_a, lru_w_x, lru_b_x,
              lru_lambda, lru_w_out,
              attn_w_qkv, attn_b_qkv, attn_sinks, attn_w_o, attn_b_o,
              ffn_w_gate, ffn_w_up, ffn_w_down,
              moe_w_router, moe_w_gate, moe_w_up, moe_w_down):
    cos, sin = rope_tables(positions)
    h = x
    for i in range(DEPTH):
        j = i // 2
        hn = rmsnorm(h, norm_mix[i])
        if i % 2 == 0:
            h = h + rglru_mixer(hn, lru_w_in[j], lru_conv_w[j], lru_conv_b[j], lru_w_a[j], lru_b_a[j],
                                lru_w_x[j], lru_b_x[j], lru_lambda[j], lru_w_out[j])
        else:
            h = h + swa_sink_mixer(hn, cos, sin, attn_w_qkv[j], attn_b_qkv[j], attn_sinks[j],
                                   attn_w_o[j], attn_b_o[j])
        hn = rmsnorm(h, norm_ffn[i])
        if i % 2 == 0:
            h = h + swiglu(hn, ffn_w_gate[j], ffn_w_up[j], ffn_w_down[j])
        else:
            h = h + moe_swiglu(hn, moe_w_router[j], moe_w_gate[j], moe_w_up[j], moe_w_down[j])
    return rmsnorm(h, norm_final)


_drawn_inputs = setup_inputs


def setup_inputs(seed=0):
    import zlib

    import numpy as np

    out = dict(_drawn_inputs(seed))
    spreads = {}
    factors = {'norm_final': 2.996, 'lru_b_a': 8.0, 'lru_b_x': 7.332, 'attn_sinks': 3.223}
    for name, (base, spread) in spreads.items():
        noise = np.random.default_rng([zlib.crc32(name.encode()), seed]).standard_normal(out[name].shape)
        drawn = base * np.exp(spread * noise) if base else spread * noise
        out[name] = __import__('jax').numpy.asarray(drawn.astype(out[name].dtype))
    for name, factor in factors.items():
        out[name] = (out[name] * factor).astype(out[name].dtype)
    return out
```

```python
from contextlib import ExitStack

import numpy as np

import concourse.bass as bass
from concourse import mybir

P = 128
D = 1024
KC = D // P
T = 256
TT = T // P
F = 3584
E = 8
TOPK = 2
CAP = 96
NH, NKV, HD = 16, 4, 64
GROUP = NH // NKV
ROT = HD // 4
THETA = 500000.0
CONV = 4
EPS = 1e-6
NEG = -1e30

CHF = 256
NCH = F // CHF
HALF = NCH // 2
SLOTS = 3 * HALF
SLOT = 2048
SCR = 4
DEPTH_EARLY = SLOTS - SCR
MAX_OVER = (TOPK * T - 1) // CAP
TILES_MORE = -(-T // CAP) - 1
NFLAG = E * TILES_MORE
NCOL = E + MAX_OVER + 2

LRU_LOADS = 13
ORDER_FFN = [13, 14, 15, 16] + list(range(13)) + [17, 18, 19, 20]
ATT_LOADS = 10
ORDER_MOE = ORDER_FFN[ATT_LOADS:17] + ORDER_FFN[:ATT_LOADS] + [17, 18, 19, 20]
FIRST_ATT = LRU_LOADS + 2 * SLOTS
FIRST_MOE = FIRST_ATT + ATT_LOADS

ALU = mybir.AluOpType
ACT = mybir.ActivationFunctionType
AX = mybir.AxisListType
F32 = mybir.dt.float32
BF16 = mybir.dt.bfloat16
I32 = mybir.dt.int32

ROWS = {}
_n = 0
for _name, _count in (("mix0", KC), ("mix1", KC), ("ffn0", KC), ("ffn1", KC), ("final", KC),
                      ("conv_w", CONV * KC), ("conv_b", KC), ("b_a", KC), ("b_x", KC), ("lam", KC),
                      ("b_qkv", 12), ("b_o", KC)):
    ROWS[_name] = (_n, _count)
    _n += _count
NROWS = _n

CONSTS = {}
_n = 0
for _name, _count in (("ident", P), ("ones", P), ("before", P), ("iota", CAP), ("earlier", E * E),
                      ("iota_over", MAX_OVER), ("thr", NFLAG), ("flag_e", NFLAG), ("inv_freq", 1),
                      ("dup0", P), ("dup1", P), ("rot", P), ("rotdup0", P), ("rotdup1", P), ("mask", 3 * P)):
    CONSTS[_name] = (_n, _count)
    _n += _count
NCONST = _n


def constant_table():
    c = np.zeros((P, NCONST), np.float32)
    i, j = np.arange(P)[:, None], np.arange(P)[None, :]

    def put(name, value):
        a, n = CONSTS[name]
        c[:, a:a + n] = value

    put("ident", i == j)
    put("ones", 1.0)
    put("before", i < j)
    put("iota", np.arange(CAP)[None])
    e = np.arange(E)
    put("earlier", (e[None, :] < e[:, None]).reshape(1, -1))
    put("iota_over", np.arange(MAX_OVER)[None])
    flag = np.arange(NFLAG)
    put("thr", (CAP * (flag % TILES_MORE + 1))[None])
    put("flag_e", (flag // TILES_MORE)[None])
    r = np.arange(P) % HD
    inv = (np.float32(THETA) ** (-np.arange(0, ROT, 2, dtype=np.float32) / np.float32(ROT))).astype(np.float32)
    put("inv_freq", np.where(r < ROT, inv[r % (ROT // 2)], 0)[:, None])
    h = ROT // 2
    src = np.where(r < h, r + h, r - h)
    sign = np.where(r < h, -1.0, 1.0) * (r < ROT)
    put("rot", np.where((i == (j // HD) * HD + src[None]) & (r[None] < ROT), sign[None], 0))
    for g in range(2):
        put(f"dup{g}", i == g * HD + j % HD)
        put(f"rotdup{g}", np.where((i == g * HD + src[None]) & (r[None] < ROT), sign[None], 0))
    causal = np.where(j <= i, 0, NEG)
    put("mask", np.concatenate([causal, np.where(j > i, 0, NEG), causal], 1))
    return c


def trunk(nc, x, positions, norm_mix, norm_ffn, norm_final, lru_w_in, lru_conv_w, lru_conv_b, lru_w_a,
          lru_b_a, lru_w_x, lru_b_x, lru_lambda, lru_w_out, attn_w_qkv, attn_b_qkv, attn_sinks, attn_w_o,
          attn_b_o, ffn_w_gate, ffn_w_up, ffn_w_down, moe_w_router, moe_w_gate, moe_w_up, moe_w_down,
          consts, out):
    with ExitStack() as ctx:
        def sb(name, shape, dt=F32):
            return ctx.enter_context(nc.sbuf_tensor(name, shape, dt))

        def sem(name):
            return ctx.enter_context(nc.semaphore(name))

        ring = sb("ring", [P, SLOTS, SLOT])
        h = sb("h", [P, KC, T])
        hn = sb("hn", [P, KC, T])
        work = sb("work", [P, 2048])
        xg_mem = sb("xg_mem", [P, KC * CAP])
        sel_mem = sb("sel_mem", [P, 4 * CAP])
        gt_mem = sb("gt_mem", [P, T])
        hact = sb("hact", [P, 2, 2, CAP])
        cst = sb("cst", [P, NCONST])
        par = sb("par", [P, NROWS])
        small = sb("small", [P, 256])
        wr = sb("wr", [P, KC, E])
        table = sb("table", [1, 2 + MAX_OVER], I32)
        ps = ctx.enter_context(nc.psum_tensor("ps", [P, 8, 512], F32))

        def const(name, rows=P):
            a, n = CONSTS[name]
            return cst[0:rows, a:a + n]

        def param(name, c=0):
            a, _ = ROWS[name]
            return par[:, a + c:a + c + 1]

        scr = ring[:, SLOTS - SCR:SLOTS, :].rearrange("p s n -> p (s n)")
        xc = scr[:, 0:2048].rearrange("p (c t) -> p c t", c=KC)
        rr = scr[:, 2048:4096].rearrange("p (c t) -> p c t", c=KC)
        aa = scr[:, 4096:6144].rearrange("p (c t) -> p c t", c=KC)
        yy = scr[:, 6144:8192].rearrange("p (c t) -> p c t", c=KC)
        x_tok = scr[:, 0:2048].rearrange("p (b d) -> p b d", b=TT)
        rows_in = scr[0:NROWS, 2048:2048 + P]
        pos_i = scr[:, 2304:2560].bitcast(I32)
        ang = scr[:, 2560:2816]
        turns = scr[:, 2816:3072]
        ang2 = scr[:, 3072:3328]
        turns2 = scr[:, 3328:3584]
        xpad = work[:, 0:2 * 260].rearrange("p (b t) -> p b t", b=2)
        igate = work[:, 520:520 + 2 * T].rearrange("p (b t) -> p b t", b=2)
        asq = work[:, 1032:1032 + 2 * T].rearrange("p (b t) -> p b t", b=2)
        sq = xg_mem[:, 0:2 * T].rearrange("p (b t) -> p b t", b=2)
        rstd = xg_mem[:, 2 * T:3 * T]
        zero = hact[0:1, :, :, :].rearrange("p a f n -> p (a f n)")[:, 0:256].bitcast(BF16)
        cosv, sinv = gt_mem[:, :], sel_mem[:, 0:T]
        q = scr[:, 0:2048].rearrange("p (c t) -> p c t", c=KC)
        kd = scr[:, 2048:3072].rearrange("p (g t) -> p g t", g=NKV)
        v_tok = scr[:, 3072:3584].rearrange("p (b n) -> p b n", b=TT)
        probs = scr[:, 3584:3584 + 3 * 384].rearrange("p (b n) -> p b n", b=3)
        probs_t = scr[:, 4736:4736 + 2 * 384].rearrange("p (b n) -> p b n", b=2)
        k_raw = scr[:, 5504:6016].rearrange("p (c t) -> p c t", c=2)
        bv_row = scr[0:1, 6016:6272]
        rope_a = scr[:, 6272:6272 + 2 * T].rearrange("p (b t) -> p b t", b=2)
        sinks = scr[:, 6784:6800]
        stat = scr[:, 6800:6800 + 2 * 64]
        heads = work[:, :].rearrange("p (c t) -> p c t", c=KC)
        ffn_h = work[:, 0:4 * T].rearrange("p (b f t) -> p b f t", b=2, f=2)
        hn_tok = work[:, :].rearrange("p (b d) -> p b d", b=TT)
        xg = xg_mem[:, :].rearrange("p (c n) -> p c n", c=KC)
        sel = sel_mem[:, 0:2 * CAP].rearrange("p (b n) -> p b n", b=TT)
        selw = sel_mem[:, 2 * CAP:4 * CAP].rearrange("p (b n) -> p b n", b=TT)
        gt = gt_mem[0:CAP, :]
        hn_flat = hn[:, :, :].rearrange("p c t -> p (c t)")
        y_sb = hn_flat[:, 0:KC * CAP].rearrange("p (c n) -> p c n", c=KC)
        y_tok = hn_flat[0:CAP, 1024:2048]
        out_tok = scr[:, 0:2048].rearrange("p (b d) -> p b d", b=TT)

        logit = small[:, 0:16].rearrange("p (b e) -> p b e", b=TT)
        top = small[:, 16:32].rearrange("p (b e) -> p b e", b=TT)
        gate = small[:, 32:40]
        chosen = small[:, 40:56].rearrange("p (b e) -> p b e", b=TT)
        order = small[:, 56:72].rearrange("p (b e) -> p b e", b=TT)
        w2nd = small[:, 72:88].rearrange("p (b e) -> p b e", b=TT)
        comb = small[:, 96:96 + TT * NCOL].rearrange("p (b n) -> p b n", b=TT)
        rank = small[:, 128:128 + TT * NCOL].rearrange("p (b n) -> p b n", b=TT)
        counts = small[:, 160:168]
        negc, posc = small[:, 168:176], small[:, 176:184]
        lt = small[:, 184:232]
        cmp_a = xg_mem[:, 0:64].rearrange("p (e j) -> p e j", e=E)
        cmp_b = xg_mem[:, 64:128].rearrange("p (e j) -> p e j", e=E)
        rt = hn_flat[:, KC * CAP:1024]
        flags, incl, excl = (rt[:, NFLAG * m:NFLAG * (m + 1)] for m in range(3))
        over_e, base, tabf = flags[:, 0:MAX_OVER], flags[:, MAX_OVER:2 * MAX_OVER], excl[0:1, 0:2 + MAX_OVER]
        hit = rt[:, 3 * NFLAG:(3 + MAX_OVER) * NFLAG].rearrange("p (o f) -> p o f", o=MAX_OVER)
        hit2_flat = rt[:, (3 + MAX_OVER) * NFLAG:(3 + 2 * MAX_OVER) * NFLAG]
        hit2 = hit2_flat.rearrange("p (o f) -> p o f", o=MAX_OVER)
        prod = hit2_flat[:, 0:MAX_OVER * E].rearrange("p (o e) -> p o e", o=MAX_OVER)
        onehot_at = (3 + 2 * MAX_OVER) * NFLAG
        onehot = rt[:, onehot_at:onehot_at + MAX_OVER * E].rearrange("p (o e) -> p o e", o=MAX_OVER)
        rank1 = lt[:, 0:16].rearrange("p (b e) -> p b e", b=TT)

        loaded = [sem(f"loaded{s}") for s in range(SLOTS)]
        used = sem("weights_used")
        x_in, cst_in, rows_sem, misc_in = sem("x_in"), sem("cst_in"), sem("rows_sem"), sem("misc_in")
        attn_in = sem("attn_in")
        out_sem = sem("out_sem")
        dve_chain, act_chain = sem("dve_chain"), sem("act_chain")
        x_turned, rows_turned, par_ready = sem("x_turned"), sem("rows_turned"), sem("par_ready")
        h_ready = sem("h_ready")
        sq_ready, sq_summed, rms_ready = sem("sq_ready"), sem("sq_summed"), sem("rms_ready")
        hn_ready = sem("hn_ready")
        x_proj, x_evac, conv_done = sem("x_proj"), sem("x_evac"), sem("conv_done")
        gates_ready, gates_evac, ix_done = sem("gates_ready"), sem("gates_evac"), sem("ix_done")
        lam_exp, negc_ready, decay_ready, tanh_ready, var_ready, root_ready = (
            sem(n) for n in ("lam_exp", "negc_ready", "decay_ready", "tanh_ready", "var_ready", "root_ready"))
        y_proj, gelu_done, z_ready, o_proj = sem("y_proj"), sem("gelu_done"), sem("z_ready"), sem("o_proj")
        angle_ready, sin_ready, zero_ready = sem("angle_ready"), sem("sin_ready"), sem("zero_ready")
        f_gu, f_silu, f_h, f_acc = sem("ffn_gu_ready"), sem("ffn_silu_done"), sem("ffn_h_done"), sem("ffn_acc_ready")
        kv_proj, k_raw_ready, kd_rot, kd_ready, v_ready = (
            sem(n) for n in ("kv_proj", "k_raw_ready", "kd_rot", "kd_ready", "v_ready"))
        q_proj, q_raw, q_rot, q_ready = sem("q_proj"), sem("q_raw"), sem("q_rot"), sem("q_ready")
        scores, masked, negmax, exp_done, norm_done = (
            sem(n) for n in ("scores", "masked", "negmax", "exp_done", "norm_done"))
        p_turned, p_copied, heads_ps, heads_ready, wo_proj = (
            sem(n) for n in ("p_turned", "p_copied", "heads_ps", "heads_ready", "wo_proj"))
        logits_ready, gap_ready, gap_exp, sel_ready, pos_ready, table_ready = (
            sem(n) for n in ("logits_ready", "gap_ready", "gap_exp", "sel_ready", "pos_ready", "table_ready"))
        hn_turned, hn_tok_ready = sem("hn_turned"), sem("hn_tok_ready")
        onehot_ready, weighted_ready, gathered, xg_ready = (
            sem(n) for n in ("onehot_ready", "weighted_ready", "gathered", "xg_ready"))
        m_gu, m_silu, m_h, y_staged = (
            sem(n) for n in ("moe_gu_ready", "moe_silu_done", "moe_h_done", "y_staged"))
        y_turned, y_tok_ready, g_turned, g_ready, scattered = (
            sem(n) for n in ("y_turned", "y_tok_ready", "g_turned", "g_ready", "scattered"))
        out_turned, out_even, out_odd = sem("out_turned"), sem("out_even"), sem("out_odd")

        slot_of = list(range(LRU_LOADS)) + 2 * ORDER_FFN + ORDER_FFN[:ATT_LOADS]
        total = {s: 0 for s in range(SLOTS)}
        arrive = []
        for k, s in enumerate(slot_of):
            total[s] += 32 if k == 4 else 16
            arrive.append(total[s])
        moe_base = dict(total)

        def columns(w, c0):
            return w[:, c0:c0 + CHF].rearrange("(k p) c -> p k c", p=P)

        def as_columns(s):
            return ring[:, s, :].rearrange("p (k c) -> p k c", k=KC)

        def as_rows(s):
            return ring[:, s, :].rearrange("p (f d) -> p f d", f=2)

        def pieces(n):
            seq = []
            for c in range(n):
                seq += [("gate", c), ("up", c)]
                if c:
                    seq.append(("down", c - 1))
            return seq + [("down", n - 1)]

        FFN_PIECES, MOE_PIECES = pieces(HALF), pieces(NCH)
        FFN_AT = {piece: j for j, piece in enumerate(FFN_PIECES)}
        MOE_AT = {piece: j for j, piece in enumerate(MOE_PIECES)}

        block = ctx.enter_context(nc.Block())

        @block.sync
        def _(sp):
            sp.dma_start(x_tok, x[0].rearrange("(b p) d -> p b d", p=P)).then_inc(x_in, 16)
            w_in, w_out = lru_w_in[0], lru_w_out[0]
            w_qkv, w_o = attn_w_qkv[0], attn_w_o[0]
            early = [("c", w_in, D + CHF * t) for t in range(4)] + [("g", None, 0)]
            early += [("c", w_in, CHF * t) for t in range(4)] + [("c", w_out, CHF * t) for t in range(4)]

            def load_early(k, kind, w, c0):
                s = slot_of[k]
                if k >= DEPTH_EARLY:
                    sp.wait_ge(used, k - DEPTH_EARLY + 1)
                if kind == "g":
                    v = ring[:, s, :].rearrange("p (m n d) -> p m n d", m=2, n=KC)
                    sp.dma_start(v[:, 0], lru_w_a[0].rearrange("n c d -> c n d")).then_inc(loaded[s], 16)
                    sp.dma_start(v[:, 1], lru_w_x[0].rearrange("n c d -> c n d")).then_inc(loaded[s], 16)
                else:
                    sp.dma_start(as_columns(s), columns(w, c0)).then_inc(loaded[s], 16)

            for k, (kind, w, c0) in enumerate(early):
                load_early(k, kind, w, c0)

            with sp.Fori(0, 2) as t:
                for j, (what, c) in enumerate(FFN_PIECES):
                    s = ORDER_FFN[j]
                    sp.wait_ge(used, SLOTS * t + max(LRU_LOADS + j - DEPTH_EARLY + 1, 1))
                    if what == "down":
                        src = ffn_w_down[0].rearrange("(u f p) d -> u p f d", p=P, f=2)[t * HALF + c]
                        sp.dma_start(as_rows(s), src).then_inc(loaded[s], 16)
                    else:
                        w = (ffn_w_gate if what == "gate" else ffn_w_up)[0]
                        src = w.rearrange("(k p) (u c) -> u p k c", p=P, c=CHF)[t * HALF + c]
                        sp.dma_start(as_columns(s), src).then_inc(loaded[s], 16)

            late = [(w_qkv, D), (w_qkv, D + CHF)] + [(w_qkv, CHF * t) for t in range(4)]
            late += [(w_o, CHF * t) for t in range(4)]
            for n, (w, c0) in enumerate(late):
                load_early(FIRST_ATT + n, "c", w, c0)

            def load_item(i, e):
                for j, (what, c) in enumerate(MOE_PIECES):
                    s = ORDER_MOE[j % SLOTS]
                    depth = DEPTH_EARLY if j < SLOTS else SLOTS
                    sp.wait_ge(used, 2 * SLOTS * i + (FIRST_MOE + j - depth + 1))
                    if what == "down":
                        src = moe_w_down[0].rearrange("e (u f p) d -> e u p f d", p=P, f=2)[e, c]
                        sp.dma_start(as_rows(s), src).then_inc(loaded[s], 16)
                    else:
                        w = (moe_w_gate if what == "gate" else moe_w_up)[0]
                        src = w.rearrange("e (k p) (u c) -> e u p k c", p=P, c=CHF)[e, c]
                        sp.dma_start(as_columns(s), src).then_inc(loaded[s], 16)

            with sp.Fori(0, E) as i:
                load_item(i, i)
            sp.wait_ge(table_ready, 1)
            n_over = sp.value_load(table[0:1, 0:1], min_val=0, max_val=MAX_OVER)
            with sp.Fori(0, MAX_OVER) as o:
                with sp.If(o < n_over):
                    e = sp.value_load(table[0:1, bass.ds(o + 2, 1)], min_val=0, max_val=E - 1)
                    load_item(o + E, e)

            for b in range(TT):
                sp.wait_ge(out_even, 2 * (b + 1))
                sp.wait_ge(out_odd, 2 * (b + 1))
                sp.dma_start(out[0].rearrange("(b p) d -> b p d", p=P)[b], out_tok[:, b, :]).then_inc(out_sem, 16)
            sp.wait_ge(out_sem, 16 * TT)

        @block.scalar
        def _(act):
            links = [0]

            def link(ins):
                links[0] += 1
                ins.then_inc(act_chain, 1)
                act.wait_ge(act_chain, links[0])

            act.dma_start(cst[:, :], consts).then_inc(cst_in, 16)
            srcs = [("mix0", norm_mix[0:1]), ("mix1", norm_mix[1:2]), ("ffn0", norm_ffn[0:1]),
                    ("ffn1", norm_ffn[1:2]), ("final", norm_final.rearrange("(a d) -> a d", a=1)),
                    ("conv_w", lru_conv_w[0]), ("conv_b", lru_conv_b), ("b_a", lru_b_a), ("b_x", lru_b_x),
                    ("lam", lru_lambda), ("b_qkv", attn_b_qkv), ("b_o", attn_b_o)]
            for name, src in srcs:
                a, n = ROWS[name]
                act.dma_start(rows_in[a:a + n, :], src.rearrange("a (c p) -> (a c) p", p=P)).then_inc(rows_sem, 16)
            act.dma_start(pos_i, positions.to_broadcast([P, T])).then_inc(misc_in, 16)
            with nc.allow_non_contiguous_dma(reason="the router's rows are 32 bytes long"):
                act.dma_start(wr[:, :, :], moe_w_router[0].rearrange("(k p) e -> p k e", p=P)).then_inc(misc_in, 16)

            def squares(n):
                for c in range(KC):
                    act.wait_ge(h_ready, KC * n + c + 1)
                    if KC * n + c >= 2:
                        act.wait_ge(sq_summed, KC * n + c - 1)
                    nc.scalar.activation(sq[:, c % 2], h[:, c], ACT.Square).then_inc(sq_ready, 1)

            def root(n, bank):
                act.wait_ge(sq_summed, KC * (n + 1))
                nc.scalar.activation(rstd, ps[:, bank, 0:T], ACT.Sqrt, bias=eps_col, scale=1.0 / D).then_inc(rms_ready, 1)

            eps_col = lt[:, 47:48]
            act.wait_ge(lam_exp, 1)
            nc.scalar.activation(lt[:, 8:16], lt[:, 0:8], ACT.Exp, scale=-1.0).then_inc(lam_exp, 1)
            act.wait_ge(angle_ready, 1)
            nc.scalar.activation(cosv, ang2, ACT.Sin).then_inc(sin_ready, 1)
            nc.scalar.activation(sinv, ang, ACT.Sin).then_inc(sin_ready, 1)
            squares(0)
            root(0, 7)

            for t in range(KC):
                act.wait_ge(x_proj, t + 1)
                if t >= 2:
                    act.wait_ge(conv_done, t - 1)
                nc.scalar.copy(xpad[:, t % 2, 3:3 + T], ps[:, t % 4, 0:T]).then_inc(x_evac, 1)
            for t in range(KC):
                act.wait_ge(gates_ready, t + 1)
                if t >= 2:
                    act.wait_ge(ix_done, t - 1)
                nc.scalar.activation(rr[:, t], ps[:, 4 + t % 2, 0:T], ACT.Sigmoid, bias=param("b_a", t)).then_inc(gates_evac, 1)
                nc.scalar.activation(igate[:, t % 2], ps[:, 4 + t % 2, T:2 * T], ACT.Sigmoid,
                                     bias=param("b_x", t)).then_inc(gates_evac, 1)
            act.wait_ge(negc_ready, 1)
            act.wait_ge(gates_evac, 2 * KC)
            for t in range(KC):
                nc.scalar.activation(aa[:, t], rr[:, t], ACT.Exp, scale=negc[:, t:t + 1]).then_inc(decay_ready, 1)
            act.wait_ge(decay_ready, KC)
            for t in range(KC):
                nc.scalar.activation(rr[:, t], rr[:, t], ACT.Tanh, scale=posc[:, t:t + 1]).then_inc(tanh_ready, 1)
            for t in range(KC):
                act.wait_ge(var_ready, t + 1)
                nc.scalar.activation(rr[:, t], rr[:, t], ACT.Sqrt).then_inc(root_ready, 1)
            for t in range(KC):
                act.wait_ge(y_proj, t + 1)
                nc.scalar.activation(yy[:, t], ps[:, t % 4, 0:T], ACT.Gelu_apprx_tanh).then_inc(gelu_done, 1)
            squares(1)
            root(1, 7)

            with act.Fori(0, 2) as t:
                for c in range(HALF):
                    for f in range(2):
                        act.wait_ge(f_gu, 2 * HALF * t + (2 * c + f + 1))
                        nc.scalar.activation(ffn_h[:, c % 2, f], ps[:, 2 * (c % 2) + f, 0:T], ACT.Silu).then_inc(f_silu, 1)
            squares(2)
            root(2, 0)

            act.wait_ge(hn_ready, 3 * KC)
            act.dma_start(sinks, attn_sinks.to_broadcast([P, NH])).then_inc(attn_in, 16)
            act.dma_start(bv_row, attn_b_qkv[:, D + NKV * HD:]).then_inc(attn_in, 16)
            for j in range(2):
                act.wait_ge(kv_proj, j + 1)
                nc.scalar.activation(k_raw[:, j], ps[:, j, 0:T], ACT.Identity, bias=param("b_qkv", 8 + j)).then_inc(k_raw_ready, 1)
            for b in range(TT):
                act.wait_ge(kv_proj, 3 + b)
                nc.scalar.copy(v_tok[:, b], ps[:, 2 + b, 0:T]).then_inc(v_ready, 1)

            def bias_q(t):
                act.wait_ge(q_proj, t + 1)
                nc.scalar.activation(q[:, t], ps[:, t % 2, 0:T], ACT.Identity, bias=param("b_qkv", t)).then_inc(q_raw, 1)

            def soften(hd):
                act.wait_ge(negmax, hd + 1)
                st = stat[:, 16 * (hd % 3):16 * (hd % 3) + 16]
                pr = probs[:, hd % 3]
                nc.scalar.activation(pr[:, 0:P], pr[:, 0:P], ACT.Exp, bias=st[:, 4:5], accum_out=st[:, 6:7]).then_inc(exp_done, 1)
                nc.scalar.activation(pr[:, P:3 * P], pr[:, P:3 * P], ACT.Exp, bias=st[:, 5:6], accum_out=st[:, 7:8]).then_inc(exp_done, 1)
                nc.scalar.activation(st[:, 8:10], st[:, 4:6], ACT.Exp, bias=sinks[:, hd:hd + 1]).then_inc(exp_done, 1)

            def copy_probs(hd):
                act.wait_ge(p_turned, hd + 1)
                nc.scalar.copy(probs_t[:, hd % 2], ps[:, 4 + hd % 2, 0:3 * P]).then_inc(p_copied, 1)

            bias_q(0)
            for t in range(KC + 1):
                if t + 1 < KC:
                    bias_q(t + 1)
                if t < KC:
                    soften(2 * t)
                    soften(2 * t + 1)
                if t >= 1:
                    for hd in (2 * t - 2, 2 * t - 1):
                        copy_probs(hd)
                    act.wait_ge(heads_ps, t)
                    nc.scalar.copy(heads[:, t - 1], ps[:, 6, 0:T]).then_inc(heads_ready, 1)
            squares(3)
            root(3, 7)
            act.wait_ge(gap_ready, 1)
            nc.scalar.activation(gate[:, 0:2], gate[:, 0:2], ACT.Exp).then_inc(gap_exp, 1)
            for g in range(4):
                act.wait_ge(hn_turned, g + 1)
                nc.scalar.copy(hn_tok[:, g // 2, (g % 2) * 512:(g % 2) * 512 + 512], ps[:, 2 + g, :]).then_inc(hn_tok_ready, 1)

            def turn_back(i):
                act.wait_ge(y_turned, 2 * i + 1)
                nc.scalar.copy(y_tok[:, 0:512], ps[0:CAP, 6, :]).then_inc(y_tok_ready, 1)

            def weights_back(i):
                act.wait_ge(g_turned, i + 1)
                nc.scalar.copy(gt, ps[0:CAP, 4, 0:T]).then_inc(g_ready, 1)

            def item(i):
                act.wait_ge(gathered, 2 * i + 1)
                nc.scalar.copy(xg[:, 0:4], ps[:, 4, 0:4 * CAP].rearrange("p (c n) -> p c n", c=4)).then_inc(xg_ready, 1)
                turn_back(i)
                for c in range(NCH):
                    act.wait_ge(m_gu, NCH * i + (c + 1))
                    g = ps[:, c % 2, 0:4 * CAP].rearrange("p (f m n) -> p f m n", f=2, m=2)
                    nc.scalar.activation(hact[:, c % 2], g[:, :, 0], ACT.Silu).then_inc(m_silu, 1)
                    if c == 0:
                        weights_back(i)
                act.wait_ge(used, 2 * SLOTS * i + (FIRST_MOE + 2 * SLOTS))
                nc.scalar.copy(y_sb[:, 0:4], ps[:, 2, 0:4 * CAP].rearrange("p (c n) -> p c n", c=4)).then_inc(y_staged, 1)

            with act.Fori(0, E) as i:
                item(i)
            act.wait_ge(table_ready, 1)
            n_over = act.value_load(table[0:1, 0:1], min_val=0, max_val=MAX_OVER)
            with act.Fori(0, MAX_OVER) as o:
                with act.If(o < n_over):
                    item(o + E)
            turn_back(n_over + E)
            weights_back(n_over + E)
            squares(4)
            root(4, 0)
            for g in range(1, 8, 2):
                act.wait_ge(out_turned, g + 1)
                nc.scalar.copy(out_tok[:, g // 4, (g % 4) * 256:(g % 4) * 256 + 256], ps[:, g, 0:256]).then_inc(out_odd, 1)

        @block.vector
        def _(dve):
            links = [0]

            def link(ins):
                links[0] += 1
                ins.then_inc(dve_chain, 1)
                dve.wait_ge(dve_chain, links[0])

            V = nc.vector
            V.memset(zero[:, :], 0.0).then_inc(zero_ready, 1)
            for b in range(2):
                V.memset(xpad[:, b, 0:3], 0.0).then_inc(zero_ready, 1)
            V.memset(small[:, 96:160], 0.0).then_inc(zero_ready, 1)
            dve.wait_ge(rows_turned, 1)
            link(V.tensor_copy(par[:, :], ps[:, 4, 0:NROWS]))
            par_ready_inc = V.memset(lt[:, 47:48], EPS)
            link(par_ready_inc)
            a, n = ROWS["lam"]
            lam = par[:, a:a + n]
            link(V.tensor_scalar(lt[:, 16:24], lam, -1.0, None, ALU.mult))
            V.tensor_tensor(lt[:, 0:8], lam, lt[:, 16:24], ALU.max).then_inc(lam_exp, 1)
            dve.wait_ge(cst_in, 16)
            dve.wait_ge(misc_in, 32)
            link(V.tensor_copy(ang, pos_i))
            link(V.tensor_scalar(ang, ang, const("inv_freq"), None, ALU.mult))
            magic = 1.5 * 2.0 ** 23
            rest, parts = 2 * np.pi, []
            for _ in range(3):
                unit = 2.0 ** (np.floor(np.log2(rest)) - 7)
                parts.append(float(np.floor(rest / unit) * unit))
                rest -= parts[-1]
            parts.append(float(rest))
            link(V.tensor_scalar(turns, ang, 1.0 / (2 * np.pi), None, ALU.mult))
            link(V.tensor_scalar(turns2, turns, 0.25, magic, ALU.add, ALU.add))
            link(V.tensor_scalar(turns, turns, magic, None, ALU.add))
            link(V.tensor_scalar(turns2, turns2, -magic, None, ALU.add))
            link(V.tensor_scalar(turns, turns, -magic, None, ALU.add))
            link(V.scalar_tensor_tensor(out=ang2, in0=turns2, scalar=-parts[0], in1=ang, op0=ALU.mult, op1=ALU.add))
            link(V.scalar_tensor_tensor(out=ang, in0=turns, scalar=-parts[0], in1=ang, op0=ALU.mult, op1=ALU.add))
            for part in parts[1:]:
                link(V.scalar_tensor_tensor(out=ang2, in0=turns2, scalar=-part, in1=ang2, op0=ALU.mult, op1=ALU.add))
                link(V.scalar_tensor_tensor(out=ang, in0=turns, scalar=-part, in1=ang, op0=ALU.mult, op1=ALU.add))
            pi = float(np.nextafter(np.float32(np.pi), np.float32(0)))
            link(V.tensor_scalar(ang2, ang2, np.pi / 2, pi, ALU.add, ALU.min))
            link(V.tensor_scalar(ang2, ang2, -pi, None, ALU.max))
            V.tensor_scalar(ang, ang, pi, -pi, ALU.min, ALU.max).then_inc(angle_ready, 1)
            for c in range(KC):
                dve.wait_ge(x_turned, c // 2 + 1)
                V.tensor_copy(h[:, c], ps[:, c // 2, (c % 2) * T:(c % 2) * T + T]).then_inc(h_ready, 1)
            dve.wait_ge(lam_exp, 2)
            w, u, u2, s_ = lt[:, 8:16], lt[:, 24:32], lt[:, 32:40], negc
            link(V.tensor_scalar(u, w, 2.0, None, ALU.add))
            link(V.reciprocal(u2, u))
            link(V.tensor_tensor(u, w, u2, ALU.mult))
            link(V.tensor_tensor(u2, u, u, ALU.mult))
            link(V.memset(s_, 1.0 / 17))
            for m in range(15, 0, -2):
                link(V.tensor_tensor(s_, s_, u2, ALU.mult))
                link(V.tensor_scalar(s_, s_, 1.0 / m, None, ALU.add))
            link(V.tensor_tensor(s_, s_, u, ALU.mult))
            link(V.tensor_scalar(s_, s_, 2.0, None, ALU.mult))
            link(V.tensor_scalar(lt[:, 16:24], lt[:, 16:24], 0.0, None, ALU.max))
            link(V.tensor_tensor(s_, s_, lt[:, 16:24], ALU.add))
            link(V.tensor_scalar(posc, s_, 8.0, None, ALU.mult))
            V.tensor_scalar(negc, s_, -8.0, None, ALU.mult).then_inc(negc_ready, 1)

            def normed(n, weight):
                dve.wait_ge(rms_ready, n + 1)
                link(V.reciprocal(rstd, rstd))
                for c in range(KC):
                    V.scalar_tensor_tensor(out=hn[:, c], in0=h[:, c], scalar=param(weight, c), in1=rstd,
                                           op0=ALU.mult, op1=ALU.mult).then_inc(hn_ready, 1)

            normed(0, "mix0")
            dve.wait_ge(zero_ready, 4)
            for t in range(KC):
                dve.wait_ge(x_evac, t + 1)
                xp = xpad[:, t % 2]
                link(V.tensor_scalar(xc[:, t], xp[:, 0:T], param("conv_w", t), param("conv_b", t), ALU.mult, ALU.add))
                for k in range(1, CONV):
                    ins = V.scalar_tensor_tensor(out=xc[:, t], in0=xp[:, k:k + T], scalar=param("conv_w", KC * k + t),
                                                 in1=xc[:, t], op0=ALU.mult, op1=ALU.add)
                    if k < CONV - 1:
                        link(ins)
                    else:
                        ins.then_inc(conv_done, 1)
            dve.wait_ge(conv_done, KC)
            for t in range(KC):
                dve.wait_ge(gates_evac, 2 * t + 2)
                V.tensor_tensor(xc[:, t], igate[:, t % 2], xc[:, t], ALU.mult).then_inc(ix_done, 1)
            for t in range(KC):
                dve.wait_ge(tanh_ready, t + 1)
                link(V.tensor_tensor(asq[:, t % 2], aa[:, t], aa[:, t], ALU.mult))
                V.scalar_tensor_tensor(out=rr[:, t], in0=asq[:, t % 2], scalar=1.0, in1=rr[:, t],
                                       op0=ALU.add, op1=ALU.mult).then_inc(var_ready, 1)
            dve.wait_ge(ix_done, KC)
            for t in range(KC):
                dve.wait_ge(root_ready, t + 1)
                link(V.tensor_tensor(xc[:, t], rr[:, t], xc[:, t], ALU.mult))
                link(V.tensor_tensor_scan(rr[:, t], aa[:, t], xc[:, t], 0.0, ALU.mult, ALU.add))
                dve.wait_ge(gelu_done, t + 1)
                V.tensor_tensor(yy[:, t], rr[:, t], yy[:, t], ALU.mult).then_inc(z_ready, 1)
            for c in range(KC):
                dve.wait_ge(o_proj, c + 1)
                V.tensor_tensor(h[:, c], ps[:, c % 4, 0:T], h[:, c], ALU.add).then_inc(h_ready, 1)
            dve.wait_ge(h_ready, 2 * KC)
            normed(1, "ffn0")
            with dve.Fori(0, 2) as t:
                for c in range(HALF):
                    for f in range(2):
                        dve.wait_ge(f_silu, 2 * HALF * t + (2 * c + f + 1))
                        hh = ffn_h[:, c % 2, f]
                        V.tensor_tensor(hh, ps[:, 2 * (c % 2) + f, T:2 * T], hh, ALU.mult).then_inc(f_h, 1)
            for c in range(KC):
                dve.wait_ge(f_acc, c // 2 + 1)
                V.tensor_tensor(h[:, c], ps[:, 4 + c // 2, (c % 2) * T:(c % 2) * T + T], h[:, c], ALU.add).then_inc(h_ready, 1)
            dve.wait_ge(h_ready, 3 * KC)
            normed(2, "mix1")
            dve.wait_ge(sin_ready, 2)
            for g in range(NKV):
                dve.wait_ge(kd_rot, g + 1)
                link(V.tensor_tensor(rope_a[:, g % 2], ps[:, 4 + g, T:2 * T], sinv, ALU.mult))
                link(V.tensor_tensor(kd[:, g], ps[:, 4 + g, 0:T], cosv, ALU.mult))
                V.tensor_tensor(kd[:, g], kd[:, g], rope_a[:, g % 2], ALU.add).then_inc(kd_ready, 1)
            dve.wait_ge(kd_ready, NKV)

            def rope_q(t):
                dve.wait_ge(q_rot, t + 1)
                link(V.tensor_tensor(rope_a[:, t % 2], ps[:, 2 + t % 2, 0:T], sinv, ALU.mult))
                link(V.tensor_tensor(q[:, t], q[:, t], cosv, ALU.mult))
                ins = V.tensor_tensor(q[:, t], q[:, t], rope_a[:, t % 2], ALU.add)
                ins.then_inc(q_ready, 1)

            def row_max(hd):
                dve.wait_ge(scores, hd + 1)
                if hd >= 3:
                    dve.wait_ge(p_turned, hd - 2)
                st = stat[:, 16 * (hd % 3):16 * (hd % 3) + 16]
                pr = probs[:, hd % 3]
                link(V.scalar_tensor_tensor(out=pr, in0=ps[:, SCORE_BANK[hd % 2], 0:3 * P], scalar=HD ** -0.5,
                                            in1=const("mask"), op0=ALU.mult, op1=ALU.add))
                V.tensor_reduce(st[:, 0:1], pr[:, 0:P], AX.X, ALU.max)
                link(V.tensor_reduce(st[:, 1:2], pr[:, P:3 * P], AX.X, ALU.max))
                V.tensor_scalar(st[:, 4:6], st[:, 0:2], sinks[:, hd:hd + 1], -1.0, ALU.max, ALU.mult).then_inc(negmax, 1)

            def normalise(hd):
                dve.wait_ge(exp_done, 3 * hd + 3)
                st = stat[:, 16 * (hd % 3):16 * (hd % 3) + 16]
                pr = probs[:, hd % 3]
                link(V.tensor_tensor(st[:, 10:12], st[:, 6:8], st[:, 8:10], ALU.add))
                link(V.reciprocal(st[:, 12:14], st[:, 10:12]))
                link(V.tensor_scalar(pr[:, 0:P], pr[:, 0:P], st[:, 12:13], None, ALU.mult))
                V.tensor_scalar(pr[:, P:3 * P], pr[:, P:3 * P], st[:, 13:14], None, ALU.mult).then_inc(norm_done, 1)

            SCORE_BANK = (7, 3)
            dve.wait_ge(attn_in, 32)
            rope_q(0)
            for t in range(KC):
                row_max(2 * t)
                row_max(2 * t + 1)
                if t + 1 < KC:
                    rope_q(t + 1)
                normalise(2 * t)
                normalise(2 * t + 1)
            for c in range(KC):
                dve.wait_ge(wo_proj, c + 1)
                V.scalar_tensor_tensor(out=h[:, c], in0=ps[:, c % 4, 0:T], scalar=param("b_o", c), in1=h[:, c],
                                       op0=ALU.add, op1=ALU.add).then_inc(h_ready, 1)
            dve.wait_ge(h_ready, 4 * KC)
            normed(3, "ffn1")

            dve.wait_ge(logits_ready, 1)
            link(V.tensor_copy(logit, ps[:, 0, 0:16].rearrange("p (b e) -> p b e", b=TT)))
            for b in range(TT):
                link(V.max(top[:, b], logit[:, b]))
                V.tensor_tensor(gate[:, b:b + 1], top[:, b, 1:2], top[:, b, 0:1], ALU.subtract).then_inc(gap_ready if b else dve_chain, 1)
                if not b:
                    links[0] += 1
            for b in range(TT):
                each = logit[:, b].unsqueeze(1).to_broadcast([P, E, E])
                own = logit[:, b].unsqueeze(2).to_broadcast([P, E, E])
                V.tensor_tensor(cmp_a, each, own, ALU.is_gt).then_inc(dve_chain, 1)
                link(V.tensor_tensor(cmp_b, each, own, ALU.is_equal))
                links[0] += 1
                dve.wait_ge(dve_chain, links[0])
                link(V.tensor_tensor(cmp_b, cmp_b, const("earlier").rearrange("p (e j) -> p e j", e=E), ALU.mult))
                link(V.tensor_tensor(cmp_a, cmp_a, cmp_b, ALU.add))
                link(V.tensor_reduce(order[:, b], cmp_a, AX.X, ALU.add))
            V.tensor_scalar(chosen, order, float(TOPK), None, ALU.is_lt).then_inc(sel_ready, 1)
            dve.wait_ge(gap_exp, 1)
            link(V.tensor_scalar(gate[:, 2:4], gate[:, 0:2], 1.0, None, ALU.add))
            link(V.reciprocal(gate[:, 4:6], gate[:, 2:4]))
            link(V.tensor_tensor(gate[:, 6:8], gate[:, 4:6], gate[:, 0:2], ALU.mult))
            for b in range(TT):
                link(V.tensor_scalar(w2nd[:, b], order[:, b], 1.0, gate[:, 6 + b:7 + b], ALU.is_equal, ALU.mult))
                link(V.tensor_scalar(comb[:, b, 1:1 + E], order[:, b], 0.0, gate[:, 4 + b:5 + b], ALU.is_equal, ALU.mult))
                link(V.tensor_tensor(comb[:, b, 1:1 + E], comb[:, b, 1:1 + E], w2nd[:, b], ALU.add))
            dve.wait_ge(pos_ready, 1)
            link(V.scalar_tensor_tensor(out=rank1, in0=ps[:, 1, 0:16].rearrange("p (b e) -> p b e", b=TT), scalar=1.0,
                                        in1=chosen, op0=ALU.add, op1=ALU.mult))
            link(V.tensor_copy(counts, ps[:, 1, 16:24]))
            link(V.tensor_scalar(rank[:, :, 0:1], rank[:, :, 0:1], -1.0, None, ALU.add))
            link(V.tensor_scalar(rank[:, :, NCOL - 1:NCOL], rank[:, :, NCOL - 1:NCOL], -1.0, None, ALU.add))
            link(V.tensor_scalar(rank[:, :, 1:1 + E], rank1, -1.0, None, ALU.add))
            for b in range(TT):
                V.tensor_scalar(sel[:, b], const("iota"), rank[:, b, 1:2], None, ALU.is_equal).then_inc(onehot_ready, 1)
                V.tensor_scalar(selw[:, b], const("iota"), rank[:, b, 0:1], comb[:, b, 0:1], ALU.is_equal, ALU.mult).then_inc(weighted_ready, 1)
            dve.wait_ge(hn_turned, 4)
            many = counts.unsqueeze(2).to_broadcast([P, E, TILES_MORE])
            f3 = flags.rearrange("p (e t) -> p e t", e=E)
            link(V.tensor_tensor(f3, many, const("thr").rearrange("p (e t) -> p e t", e=E), ALU.is_gt))
            link(V.tensor_tensor_scan(incl, const("ones")[:, 0:NFLAG], flags, 0.0, ALU.mult, ALU.add))
            link(V.tensor_tensor(excl, incl, flags, ALU.subtract))
            shape = [P, MAX_OVER, NFLAG]
            link(V.tensor_tensor(hit, excl.unsqueeze(1).to_broadcast(shape), const("iota_over").unsqueeze(2).to_broadcast(shape), ALU.is_equal))
            link(V.tensor_tensor(hit, hit, flags.unsqueeze(1).to_broadcast(shape), ALU.mult))
            link(V.tensor_tensor(hit2, hit, const("flag_e").unsqueeze(1).to_broadcast(shape), ALU.mult))
            link(V.tensor_reduce(over_e, hit2, AX.X, ALU.add))
            link(V.tensor_tensor(hit2, hit, const("thr").unsqueeze(1).to_broadcast(shape), ALU.mult))
            link(V.tensor_reduce(base, hit2, AX.X, ALU.add))
            link(V.tensor_reduce(onehot, hit.rearrange("p o (e t) -> p o e t", e=E), AX.X, ALU.add))
            oe = [P, MAX_OVER, E]
            for b in range(TT):
                link(V.tensor_tensor(prod, onehot, rank1[:, b].unsqueeze(1).to_broadcast(oe), ALU.mult))
                link(V.tensor_reduce(rank[:, b, 1 + E:1 + E + MAX_OVER], prod, AX.X, ALU.add))
                link(V.scalar_tensor_tensor(out=rank[:, b, 1 + E:1 + E + MAX_OVER], in0=rank[:, b, 1 + E:1 + E + MAX_OVER],
                                            scalar=-1.0, in1=base, op0=ALU.add, op1=ALU.subtract))
                link(V.tensor_tensor(prod, onehot, comb[:, b, 1:1 + E].unsqueeze(1).to_broadcast(oe), ALU.mult))
                link(V.tensor_reduce(comb[:, b, 1 + E:1 + E + MAX_OVER], prod, AX.X, ALU.add))
            link(V.tensor_copy(tabf[:, 0:1], incl[0:1, NFLAG - 1:NFLAG]))
            link(V.tensor_copy(tabf[:, 1:2], incl[0:1, NFLAG - 1:NFLAG]))
            link(V.tensor_copy(tabf[:, 2:2 + MAX_OVER], over_e[0:1, :]))
            link(V.tensor_copy(table[:, :], tabf))
            V.memset(y_sb, 0.0).then_inc(y_staged, 1)
            dve.wait_ge(y_staged, 1)
            V.memset(hact[:, 0, 0, 0:1], 0.0).then_inc(table_ready, 1)

            def turn_back(i):
                dve.wait_ge(y_turned, 2 * i + 2)
                V.tensor_copy(y_tok[:, 512:1024], ps[0:CAP, 7, :]).then_inc(y_tok_ready, 1)

            def add_back(i, m):
                dve.wait_ge(scattered, 4 * i + (m + 1))
                hh = h[:, 2 * m:2 * m + 2, :].rearrange("p c t -> p (c t)")
                return V.tensor_tensor(hh, ps[:, SCATTER_BANK[m], :], hh, ALU.add)

            def item(i):
                dve.wait_ge(gathered, 2 * i + 2)
                V.tensor_copy(xg[:, 4:8], ps[:, 5, 0:4 * CAP].rearrange("p (c n) -> p c n", c=4)).then_inc(xg_ready, 1)
                turn_back(i)
                for c in range(NCH):
                    dve.wait_ge(m_silu, NCH * i + (c + 1))
                    g = ps[:, c % 2, 0:4 * CAP].rearrange("p (f m n) -> p f m n", f=2, m=2)
                    V.tensor_tensor(hact[:, c % 2], g[:, :, 1], hact[:, c % 2], ALU.mult).then_inc(m_h, 1)
                    if c in (2, 4):
                        add_back(i, c - 2)
                        add_back(i, c - 1)
                    if c == 7:
                        for b in range(TT):
                            V.tensor_scalar(selw[:, b], const("iota"), rank[:, b, bass.ds(i + 1, 1)],
                                            comb[:, b, bass.ds(i + 1, 1)], ALU.is_equal, ALU.mult).then_inc(weighted_ready, 1)
                            V.tensor_scalar(sel[:, b], const("iota"), rank[:, b, bass.ds(i + 2, 1)], None,
                                            ALU.is_equal).then_inc(onehot_ready, 1)
                dve.wait_ge(used, 2 * SLOTS * i + (FIRST_MOE + 2 * SLOTS))
                V.tensor_copy(y_sb[:, 4:8], ps[:, 3, 0:4 * CAP].rearrange("p (c n) -> p c n", c=4)).then_inc(y_staged, 1)

            SCATTER_BANK = (5, 6, 7, 4)
            with dve.Fori(0, E) as i:
                item(i)
            n_over = dve.value_load(table[0:1, 0:1], min_val=0, max_val=MAX_OVER)
            with dve.Fori(0, MAX_OVER) as o:
                with dve.If(o < n_over):
                    item(o + E)
            last = n_over + E
            turn_back(last)
            for m in range(4):
                add_back(last, m).then_inc(h_ready, 2)
            dve.wait_ge(h_ready, 5 * KC)
            normed(4, "final")
            for g in range(0, 8, 2):
                dve.wait_ge(out_turned, g + 1)
                V.tensor_copy(out_tok[:, g // 4, (g % 4) * 256:(g % 4) * 256 + 256], ps[:, g, 0:256]).then_inc(out_even, 1)

        @block.tensor
        def _(pe):
            ident = const("ident")

            def arrived(k):
                pe.wait_ge(loaded[slot_of[k]], arrive[k])

            def sum_square(n, c, bank):
                pe.wait_ge(sq_ready, KC * n + c + 1)
                mm = nc.tensor.matmul(ps[:, bank, 0:T], const("ones"), sq[:, c % 2], start=(c == 0), stop=(c == KC - 1))
                mm.then_inc(sq_summed, 1)

            def tile(bank, w, col, rhs, waits=None, c0=0, frees=False):
                for k in range(KC):
                    if waits:
                        waits(k)
                    mm = nc.tensor.matmul(ps[:, bank, c0:c0 + T], w[:, k, col:col + P], rhs[:, k], start=(k == 0), stop=(k == KC - 1))
                    if frees and k == 0:
                        mm.then_inc(used, 1)
                return mm

            pe.wait_ge(cst_in, 16)
            pe.wait_ge(rows_sem, 16 * 12)
            nc.tensor.transpose(ps[:, 4, 0:NROWS], rows_in, cst[0:NROWS, 0:NROWS]).then_inc(rows_turned, 1)
            pe.wait_ge(x_in, 16)
            for c in range(KC):
                for b in range(TT):
                    col = (c % 2) * T + b * P
                    mm = nc.tensor.transpose(ps[:, c // 2, col:col + P], x_tok[:, b, c * P:(c + 1) * P], ident)
                if c % 2:
                    mm.then_inc(x_turned, 1)
            for c in range(KC):
                sum_square(0, c, 7)

            for t in range(KC):
                arrived(t // 2)
                if t >= 4:
                    pe.wait_ge(x_evac, t - 3)
                mm = tile(t % 4, as_columns(slot_of[t // 2]), (t % 2) * P, hn,
                          (lambda k: pe.wait_ge(hn_ready, k + 1)) if t == 0 else None, frees=t in (2, 4, 6))
                mm.then_inc(x_proj, 1)
            arrived(4)
            wg = ring[:, slot_of[4], :].rearrange("p (m n d) -> p m n d", m=2, n=KC)
            for t in range(KC):
                pe.wait_ge(conv_done, t + 1)
                if t >= 2:
                    pe.wait_ge(gates_evac, 2 * (t - 1))
                for m in range(2):
                    mm = nc.tensor.matmul(ps[:, 4 + t % 2, m * T:(m + 1) * T], wg[:, m, t], xc[:, t], start=True, stop=True)
                    if t == 0 and m == 0:
                        mm.then_inc(used, 1)
                mm.then_inc(gates_ready, 1)
            pe.wait_ge(x_evac, KC)
            for t in range(KC):
                arrived(5 + t // 2)
                if t >= 4:
                    pe.wait_ge(gelu_done, t - 3)
                mm = tile(t % 4, as_columns(slot_of[5 + t // 2]), (t % 2) * P, hn, frees=t % 2 == 0)
                mm.then_inc(y_proj, 1)
            for t in range(KC):
                arrived(9 + t // 2)
                if t >= 4:
                    pe.wait_ge(h_ready, KC + t - 3)
                else:
                    pe.wait_ge(gelu_done, t + 5)
                mm = tile(t % 4, as_columns(slot_of[9 + t // 2]), (t % 2) * P, yy,
                          (lambda k: pe.wait_ge(z_ready, k + 1)) if t == 0 else None, frees=t % 2 == 0)
                mm.then_inc(o_proj, 1)
                if t >= 1:
                    sum_square(1, t - 1, 7)
            sum_square(1, KC - 1, 7)

            def open_banks(banks):
                pe.wait_ge(zero_ready, 1)
                for b in banks:
                    mm = nc.tensor.matmul(ps[:, b, :], zero[:, 0:P], zero[:, :], start=True, stop=True)
                mm.then_inc(used, 1)

            pe.wait_ge(rms_ready, 2)
            open_banks(range(4, 8))
            pe.wait_ge(hn_ready, 2 * KC)

            with pe.Fori(0, 2) as t:
                def ffn_arrived(piece):
                    j = FFN_AT[piece]
                    s = ORDER_FFN[j]
                    pe.wait_ge(loaded[s], 16 * t + arrive[LRU_LOADS + j])
                    return s

                def ffn_down(c):
                    s = ffn_arrived(("down", c))
                    for f in range(2):
                        pe.wait_ge(f_h, 2 * HALF * t + (2 * c + f + 1))
                        for d in range(KC):
                            mm = nc.tensor.matmul(ps[:, 4 + d // 2, (d % 2) * T:(d % 2 + 1) * T], as_rows(s)[:, f, d * P:(d + 1) * P],
                                                  ffn_h[:, c % 2, f], start=False, stop=False, skip_group_check=True)
                            if f == 0 and d == 0 and c < HALF - 1:
                                mm.then_inc(used, 1)
                    mm.then_inc(used, 1)

                for c in range(HALF):
                    slots = [ffn_arrived((m, c)) for m in ("gate", "up")]
                    for f in range(2):
                        for m in range(2):
                            mm = tile(2 * (c % 2) + f, as_columns(slots[m]), f * P, hn, c0=m * T, frees=(c, f, m) == (1, 0, 0))
                            if f == 1 and m == 0:
                                mm.then_inc(used, 1)
                        mm.then_inc(f_gu, 1)
                    if c:
                        ffn_down(c - 1)
                ffn_down(HALF - 1)
            for b in range(4, 8):
                nc.tensor.matmul(ps[:, b, :], zero[:, 0:P], zero[:, :], start=False, stop=True, skip_group_check=True).then_inc(f_acc, 1)
            for c in range(KC):
                sum_square(2, c, 0)

            pe.wait_ge(rms_ready, 3)
            pe.wait_ge(hn_ready, 3 * KC)
            arrived(FIRST_ATT)
            wk = as_columns(slot_of[FIRST_ATT])
            for j in range(2):
                mm = tile(j, wk, j * P, hn)
                mm.then_inc(kv_proj, 1)
            arrived(FIRST_ATT + 1)
            wv = as_columns(slot_of[FIRST_ATT + 1])
            pe.wait_ge(attn_in, 32)
            for b in range(TT):
                mm = nc.tensor.matmul(ps[:, 2 + b, 0:T], const("ones", 1), bv_row, start=True, stop=False)
                if b == 0:
                    mm.then_inc(used, 1)
                for k in range(KC):
                    mm = nc.tensor.matmul(ps[:, 2 + b, 0:T], hn[:, k, b * P:(b + 1) * P], wv[:, k, :], start=False, stop=(k == KC - 1))
                mm.then_inc(kv_proj, 1)
            pe.wait_ge(k_raw_ready, 2)
            for g in range(NKV):
                mm = nc.tensor.matmul(ps[:, 4 + g, 0:T], const(f"dup{g % 2}"), k_raw[:, g // 2], start=True, stop=True)
                if g == 0:
                    mm.then_inc(used, 1)
                nc.tensor.matmul(ps[:, 4 + g, T:2 * T], const(f"rotdup{g % 2}"), k_raw[:, g // 2], start=True, stop=True).then_inc(kd_rot, 1)
            pe.wait_ge(v_ready, 2)

            SCORE_BANK = (7, 3)

            def project_q(t):
                arrived(FIRST_ATT + 2 + t // 2)
                if t >= 2:
                    pe.wait_ge(q_raw, t - 1)
                mm = tile(t % 2, as_columns(slot_of[FIRST_ATT + 2 + t // 2]), (t % 2) * P, hn, frees=t in (2, 4, 6))
                mm.then_inc(q_proj, 1)

            def rotate_q(t):
                pe.wait_ge(q_raw, t + 1)
                if t >= 1:
                    pe.wait_ge(negmax, 2 * t)
                nc.tensor.matmul(ps[:, 2 + t % 2, 0:T], const("rot"), q[:, t], start=True, stop=True).then_inc(q_rot, 1)

            def score(hd):
                pe.wait_ge(q_ready, hd // 2 + 1)
                if hd >= 2:
                    pe.wait_ge(negmax, hd - 1)
                o, t, g = (hd % 2) * HD, hd // 2, hd // GROUP
                bank = SCORE_BANK[hd % 2]
                mm = nc.tensor.matmul(ps[:, bank, 0:P], q[o:o + HD, t, 0:P], kd[o:o + HD, g, 0:P], start=True, stop=True)
                if hd == 2 * (KC - 1):
                    mm.then_inc(used, 1)
                nc.tensor.matmul(ps[:, bank, P:3 * P], q[o:o + HD, t, P:2 * P], kd[o:o + HD, g, :], start=True, stop=True).then_inc(scores, 1)

            def turn_probs(hd):
                pe.wait_ge(norm_done, hd + 1)
                if hd >= 2:
                    pe.wait_ge(p_copied, hd - 1)
                for m in range(3):
                    mm = nc.tensor.transpose(ps[:, 4 + hd % 2, m * P:(m + 1) * P], probs[:, hd % 3, m * P:(m + 1) * P], ident)
                mm.then_inc(p_turned, 1)

            def weigh_values(hd):
                pe.wait_ge(p_copied, hd + 1)
                if hd >= 2:
                    pe.wait_ge(heads_ready, hd // 2)
                o, g, pt = (hd % 2) * HD, hd // GROUP, probs_t[:, hd % 2]
                v = [v_tok[:, b, g * HD:(g + 1) * HD] for b in range(TT)]
                nc.tensor.matmul(ps[o:o + HD, 6, 0:P], v[0], pt[:, 0:P], start=True, stop=True)
                nc.tensor.matmul(ps[o:o + HD, 6, P:2 * P], v[0], pt[:, P:2 * P], start=True, stop=False)
                mm = nc.tensor.matmul(ps[o:o + HD, 6, P:2 * P], v[1], pt[:, 2 * P:3 * P], start=False, stop=True)
                if hd % 2:
                    mm.then_inc(heads_ps, 1)

            pe.wait_ge(kd_ready, NKV)
            project_q(0)
            rotate_q(0)
            for t in range(KC + 1):
                if t + 1 < KC:
                    project_q(t + 1)
                if t < KC:
                    score(2 * t)
                    score(2 * t + 1)
                if t >= 1:
                    turn_probs(2 * t - 2)
                    turn_probs(2 * t - 1)
                if t + 1 < KC:
                    rotate_q(t + 1)
                if t >= 1:
                    weigh_values(2 * t - 2)
                    weigh_values(2 * t - 1)
            for t in range(KC):
                arrived(FIRST_ATT + 6 + t // 2)
                if t >= 4:
                    pe.wait_ge(h_ready, 3 * KC + t - 3)
                mm = tile(t % 4, as_columns(slot_of[FIRST_ATT + 6 + t // 2]), (t % 2) * P, heads,
                          (lambda k: pe.wait_ge(heads_ready, k + 1)) if t == 0 else None, frees=t in (2, 4, 6))
                mm.then_inc(wo_proj, 1)
                if t >= 1:
                    sum_square(3, t - 1, 7)
            sum_square(3, KC - 1, 7)

            pe.wait_ge(misc_in, 32)
            pe.wait_ge(hn_ready, 4 * KC)
            for b in range(TT):
                for k in range(KC):
                    mm = nc.tensor.matmul(ps[:, 0, b * E:(b + 1) * E], hn[:, k, b * P:(b + 1) * P], wr[:, k, :], start=(k == 0), stop=(k == KC - 1))
                    if b == 0 and k == 0:
                        mm.then_inc(used, 1)
            mm.then_inc(logits_ready, 1)
            for g in range(4):
                for m in range(4):
                    c = 4 * (g % 2) + m
                    mm = nc.tensor.transpose(ps[:, 2 + g, m * P:(m + 1) * P], hn[:, c, (g // 2) * P:(g // 2 + 1) * P], ident)
                mm.then_inc(hn_turned, 1)
            pe.wait_ge(sel_ready, 1)
            nc.tensor.matmul(ps[:, 1, 0:E], const("before"), chosen[:, 0], start=True, stop=True)
            nc.tensor.matmul(ps[:, 1, E:2 * E], const("before"), chosen[:, 1], start=True, stop=False)
            nc.tensor.matmul(ps[:, 1, E:2 * E], const("ones"), chosen[:, 0], start=False, stop=True)
            nc.tensor.matmul(ps[:, 1, 2 * E:3 * E], const("ones"), chosen[:, 0], start=True, stop=False)
            nc.tensor.matmul(ps[:, 1, 2 * E:3 * E], const("ones"), chosen[:, 1], start=False, stop=True).then_inc(pos_ready, 1)

            SCATTER_BANK = (5, 6, 7, 4)

            def turn_back(i):
                pe.wait_ge(y_staged, 2 * i + 1)
                for g in range(2):
                    for m in range(4):
                        mm = nc.tensor.transpose(ps[0:CAP, 6 + g, m * P:(m + 1) * P], y_sb[:, 4 * g + m], ident)
                    mm.then_inc(y_turned, 1)

            def weights_back(i, in_item=True):
                pe.wait_ge(weighted_ready, 2 * i + 2)
                for b in range(TT):
                    mm = nc.tensor.transpose(ps[0:CAP, 4, b * P:(b + 1) * P], selw[:, b], ident)
                    if b == 0 and in_item:
                        mm.then_inc(used, 1)
                mm.then_inc(g_turned, 1)

            def scatter(i, m):
                if m == 0:
                    pe.wait_ge(g_ready, i + 1)
                    pe.wait_ge(y_tok_ready, 2 * i + 2)
                for d in (2 * m, 2 * m + 1):
                    mm = nc.tensor.matmul(ps[:, SCATTER_BANK[m], (d % 2) * T:(d % 2 + 1) * T], y_tok[:, d * P:(d + 1) * P], gt, start=True, stop=True)
                mm.then_inc(scattered, 1)

            def item(i):
                def moe_arrived(piece):
                    j = MOE_AT[piece]
                    s = ORDER_MOE[j % SLOTS]
                    pe.wait_ge(loaded[s], 32 * i + (moe_base[s] + 16 * (j // SLOTS + 1)))
                    return s

                def moe_down(c):
                    s = moe_arrived(("down", c))
                    pe.wait_ge(m_h, NCH * i + (c + 1))
                    for f in range(2):
                        for d in range(KC):
                            mm = nc.tensor.matmul(ps[:, 2 + d // 4, (d % 4) * CAP:(d % 4 + 1) * CAP], as_rows(s)[:, f, d * P:(d + 1) * P],
                                                  hact[:, c % 2, f], start=(c == 0 and f == 0 and d % 4 == 0),
                                                  stop=(c == NCH - 1 and f == 1 and d % 4 == 3), skip_group_check=True)
                            if f == 0 and d == 0 and c < NCH - 1:
                                mm.then_inc(used, 1)
                    mm.then_inc(used, 1)

                pe.wait_ge(onehot_ready, 2 * i + 2)
                for g in range(2):
                    for m in range(4):
                        c = 4 * g + m
                        for b in range(TT):
                            mm = nc.tensor.matmul(ps[:, 4 + g, m * CAP:(m + 1) * CAP], hn_tok[:, b, c * P:(c + 1) * P], sel[:, b],
                                                  start=(b == 0), stop=(b == TT - 1))
                    mm.then_inc(gathered, 1)
                turn_back(i)
                pe.wait_ge(xg_ready, 2 * i + 2)
                for c in range(NCH):
                    slots = [moe_arrived((m, c)) for m in ("gate", "up")]
                    for f in range(2):
                        for m in range(2):
                            for k in range(KC):
                                col = (2 * f + m) * CAP
                                mm = nc.tensor.matmul(ps[:, c % 2, col:col + CAP], as_columns(slots[m])[:, k, f * P:(f + 1) * P], xg[:, k],
                                                      start=(k == 0), stop=(k == KC - 1))
                            if f == 1 and m == 0:
                                mm.then_inc(used, 1)
                    mm.then_inc(m_gu, 1)
                    if c == 0:
                        weights_back(i)
                    if c:
                        moe_down(c - 1)
                    if c in (2, 4):
                        scatter(i, c - 2)
                        scatter(i, c - 1)
                moe_down(NCH - 1)

            pe.wait_ge(hn_tok_ready, 4)
            with pe.Fori(0, E) as i:
                item(i)
            pe.wait_ge(table_ready, 1)
            n_over = pe.value_load(table[0:1, 0:1], min_val=0, max_val=MAX_OVER)
            with pe.Fori(0, MAX_OVER) as o:
                with pe.If(o < n_over):
                    item(o + E)
            last = n_over + E
            turn_back(last)
            weights_back(last, in_item=False)
            for m in range(4):
                scatter(last, m)
            for c in range(KC):
                sum_square(4, c, 0)

            pe.wait_ge(hn_ready, 5 * KC)
            for g in range(8):
                for m in range(2):
                    c = 2 * (g % 4) + m
                    mm = nc.tensor.transpose(ps[:, g, m * P:(m + 1) * P], hn[:, c, (g // 4) * P:(g // 4 + 1) * P], ident)
                mm.then_inc(out_turned, 1)


_INS = ['x', 'positions', 'norm_mix', 'norm_ffn', 'norm_final', 'lru_w_in', 'lru_conv_w', 'lru_conv_b', 'lru_w_a',
        'lru_b_a', 'lru_w_x', 'lru_b_x', 'lru_lambda', 'lru_w_out', 'attn_w_qkv', 'attn_b_qkv', 'attn_sinks',
        'attn_w_o', 'attn_b_o', 'ffn_w_gate', 'ffn_w_up', 'ffn_w_down', 'moe_w_router', 'moe_w_gate', 'moe_w_up',
        'moe_w_down']


def kernel(**inputs):
    import numpy as _np
    import concourse.bacc as _bacc
    from concourse import mybir as _mybir
    from concourse.bass_utils import run_bass_kernel_spmd as _run

    nc = _bacc.Bacc("TRN2", target_bir_lowering=False, num_devices=1)
    arrays, args = {}, []
    for name in _INS:
        a = _np.ascontiguousarray(inputs[name])
        arrays[f"in_{name}"] = a
        args.append(nc.dram_tensor(f"in_{name}", a.shape, _mybir.dt.from_np(a.dtype), kind="ExternalInput").ap())
    c = constant_table()
    arrays["in_consts"] = c
    args.append(nc.dram_tensor("in_consts", c.shape, _mybir.dt.from_np(c.dtype), kind="ExternalInput").ap())
    args.append(nc.dram_tensor("out_0", (1, T, D), _mybir.dt.from_np(_np.dtype("float32")), kind="ExternalOutput").ap())
    trunk(nc, *args)
    r = _run(nc, [arrays], core_ids=[0])
    return r.results[0]["out_0"]
```

```python
from contextlib import ExitStack

import numpy as np

import concourse.bass as bass
from concourse import mybir

P = 128
D = 1024
KC = D // P
T = 256
TT = T // P
F = 3584
E = 8
TOPK = 2
CAP = 96
NH, NKV, HD = 16, 4, 64
GROUP = NH // NKV
ROT = HD // 4
THETA = 500000.0
CONV = 4
EPS = 1e-6
NEG = -1e30

CHF = 256
NCH = F // CHF
HALF = NCH // 2
SLOTS = 2 * HALF
SLOT = 2048
PARTS = 3
PIECES = 3 * NCH
MAX_OVER = (TOPK * T - 1) // CAP
TILES_MORE = -(-T // CAP) - 1
NFLAG = E * TILES_MORE
NCOL = E + MAX_OVER + 2

LRU_LOADS, ATT_LOADS = 13, 10
ORDER_FFN = [13, 0, 1, 2, 3, 4, 5]
ORDER_ATT = [6, 7, 8, 9, 10, 11, 12, 13, 0, 1]
ORDER_MOE = [2, 3, 4, 5] + ORDER_ATT
FIRST_ATT = LRU_LOADS + 2 * 3 * HALF
FIRST_MOE = FIRST_ATT + ATT_LOADS

ALU = mybir.AluOpType
ACT = mybir.ActivationFunctionType
AX = mybir.AxisListType
F32 = mybir.dt.float32
F32R = mybir.dt.float32r
BF16 = mybir.dt.bfloat16
I32 = mybir.dt.int32

ROWS = {}
_n = 0
for _name, _count in (("mix0", KC), ("mix1", KC), ("ffn0", KC), ("ffn1", KC), ("final", KC),
                      ("conv_w", CONV * KC), ("conv_b", KC), ("b_a", KC), ("b_x", KC), ("lam", KC),
                      ("b_qkv", 12), ("b_o", KC)):
    ROWS[_name] = (_n, _count)
    _n += _count
NROWS = _n

CONSTS = {}
_n = 0
for _name, _count in (("ident", P), ("ones", P), ("before", P), ("iota", CAP), ("earlier", E * E),
                      ("iota_over", MAX_OVER), ("thr", NFLAG), ("flag_e", NFLAG), ("inv_freq", 1),
                      ("dup0", P), ("dup1", P), ("rot", P), ("rotdup0", P), ("rotdup1", P), ("mask", 3 * P)):
    CONSTS[_name] = (_n, _count)
    _n += _count
NCONST = _n


def constant_table():
    c = np.zeros((P, NCONST), np.float32)
    i, j = np.arange(P)[:, None], np.arange(P)[None, :]

    def put(name, value):
        a, n = CONSTS[name]
        c[:, a:a + n] = value

    put("ident", i == j)
    put("ones", 1.0)
    put("before", i < j)
    put("iota", np.arange(CAP)[None])
    e = np.arange(E)
    put("earlier", (e[None, :] < e[:, None]).reshape(1, -1))
    put("iota_over", np.arange(MAX_OVER)[None])
    flag = np.arange(NFLAG)
    put("thr", (CAP * (flag % TILES_MORE + 1))[None])
    put("flag_e", (flag // TILES_MORE)[None])
    r = np.arange(P) % HD
    inv = (np.float32(THETA) ** (-np.arange(0, ROT, 2, dtype=np.float32) / np.float32(ROT))).astype(np.float32)
    put("inv_freq", np.where(r < ROT, inv[r % (ROT // 2)], 0)[:, None])
    h = ROT // 2
    src = np.where(r < h, r + h, r - h)
    sign = np.where(r < h, -1.0, 1.0) * (r < ROT)
    put("rot", np.where((i == (j // HD) * HD + src[None]) & (r[None] < ROT), sign[None], 0))
    for g in range(2):
        put(f"dup{g}", i == g * HD + j % HD)
        put(f"rotdup{g}", np.where((i == g * HD + src[None]) & (r[None] < ROT), sign[None], 0))
    causal = np.where(j <= i, 0, NEG)
    put("mask", np.concatenate([causal, np.where(j > i, 0, NEG), causal], 1))
    return c


def trunk(nc, x, positions, norm_mix, norm_ffn, norm_final, lru_w_in, lru_conv_w, lru_conv_b, lru_w_a,
          lru_b_a, lru_w_x, lru_b_x, lru_lambda, lru_w_out, attn_w_qkv, attn_b_qkv, attn_sinks, attn_w_o,
          attn_b_o, ffn_w_gate, ffn_w_up, ffn_w_down, moe_w_router, moe_w_gate, moe_w_up, moe_w_down,
          consts, out):
    with ExitStack() as ctx:
        def sb(name, shape, dt=F32):
            return ctx.enter_context(nc.sbuf_tensor(name, shape, dt))

        def sem(name):
            return ctx.enter_context(nc.semaphore(name))

        ring = sb("ring", [P, SLOTS, SLOT])
        h = sb("h", [P, KC, T])
        hn = sb("hn", [P, KC, T])
        work = sb("work", [P, 2048])
        xg_mem = sb("xg_mem", [P, KC * CAP])
        sel_mem = sb("sel_mem", [P, 4 * CAP])
        gt_mem = sb("gt_mem", [P, T])
        zero_mem = sb("zero_mem", [1, 512], BF16)
        xg_hi, xg_lo = sb("xg_hi", [P, KC, CAP], F32R), sb("xg_lo", [P, KC, CAP], F32R)
        ht_hi, ht_lo = sb("ht_hi", [P, 2, 2, CAP], F32R), sb("ht_lo", [P, 2, 2, CAP], F32R)
        cst = sb("cst", [P, NCONST])
        par = sb("par", [P, NROWS])
        small = sb("small", [P, 256])
        wr = sb("wr", [P, KC, E])
        table = sb("table", [1, 2 + MAX_OVER], I32)
        with nc.sbuf_tensor("scratch", [P, 4 * SLOT], F32) as scratch:
            pass
        w_hi, w_lo = sb("w_hi", [P, PARTS, SLOT], F32R), sb("w_lo", [P, PARTS, SLOT], F32R)
        ps = ctx.enter_context(nc.psum_tensor("ps", [P, 8, 512], F32))

        def const(name, rows=P):
            a, n = CONSTS[name]
            return cst[0:rows, a:a + n]

        def param(name, c=0):
            a, _ = ROWS[name]
            return par[:, a + c:a + c + 1]

        scr = scratch[:, :]
        xc = scr[:, 0:2048].rearrange("p (c t) -> p c t", c=KC)
        rr = scr[:, 2048:4096].rearrange("p (c t) -> p c t", c=KC)
        aa = scr[:, 4096:6144].rearrange("p (c t) -> p c t", c=KC)
        yy = scr[:, 6144:8192].rearrange("p (c t) -> p c t", c=KC)
        x_tok = scr[:, 0:2048].rearrange("p (b d) -> p b d", b=TT)
        rows_in = scr[0:NROWS, 2048:2048 + P]
        pos_i = scr[:, 2304:2560].bitcast(I32)
        ang = scr[:, 2560:2816]
        turns = scr[:, 2816:3072]
        ang2 = scr[:, 3072:3328]
        turns2 = scr[:, 3328:3584]
        xpad = work[:, 0:2 * 260].rearrange("p (b t) -> p b t", b=2)
        igate = work[:, 520:520 + 2 * T].rearrange("p (b t) -> p b t", b=2)
        asq = work[:, 1032:1032 + 2 * T].rearrange("p (b t) -> p b t", b=2)
        sq = xg_mem[:, 0:2 * T].rearrange("p (b t) -> p b t", b=2)
        rstd = xg_mem[:, 2 * T:3 * T]
        zero = zero_mem[:, :]
        cosv, sinv = gt_mem[:, :], sel_mem[:, 0:T]
        q = scr[:, 0:2048].rearrange("p (c t) -> p c t", c=KC)
        kd = scr[:, 2048:3072].rearrange("p (g t) -> p g t", g=NKV)
        v_tok = scr[:, 3072:3584].rearrange("p (b n) -> p b n", b=TT)
        probs = scr[:, 3584:3584 + 3 * 384].rearrange("p (b n) -> p b n", b=3)
        probs_t = scr[:, 4736:4736 + 2 * 384].rearrange("p (b n) -> p b n", b=2)
        k_raw = scr[:, 5504:6016].rearrange("p (c t) -> p c t", c=2)
        bv_row = scr[0:1, 6016:6272]
        rope_a = scr[:, 6272:6272 + 2 * T].rearrange("p (b t) -> p b t", b=2)
        sinks = scr[:, 6784:6800]
        stat = scr[:, 6800:6800 + 2 * 64]
        heads = work[:, :].rearrange("p (c t) -> p c t", c=KC)
        ffn_h = work[:, 0:4 * T].rearrange("p (b f t) -> p b f t", b=2, f=2)
        hn_tok = work[:, :].rearrange("p (b d) -> p b d", b=TT)
        sel = sel_mem[:, 0:2 * CAP].rearrange("p (b n) -> p b n", b=TT)
        selw = sel_mem[:, 2 * CAP:4 * CAP].rearrange("p (b n) -> p b n", b=TT)
        gt = gt_mem[0:CAP, :]
        hn_flat = hn[:, :, :].rearrange("p c t -> p (c t)")
        h_tok = hn_flat[0:CAP, 0:2 * CHF].rearrange("p (b f) -> p b f", b=2)
        y_tok = hn_flat[0:CAP, 1024:2048]
        out_tok = work[:, :].rearrange("p (b d) -> p b d", b=TT)

        logit = small[:, 0:16].rearrange("p (b e) -> p b e", b=TT)
        top = small[:, 16:32].rearrange("p (b e) -> p b e", b=TT)
        gate = small[:, 32:40]
        chosen = small[:, 40:56].rearrange("p (b e) -> p b e", b=TT)
        order = small[:, 56:72].rearrange("p (b e) -> p b e", b=TT)
        w2nd = small[:, 72:88].rearrange("p (b e) -> p b e", b=TT)
        comb = small[:, 96:96 + TT * NCOL].rearrange("p (b n) -> p b n", b=TT)
        rank = small[:, 128:128 + TT * NCOL].rearrange("p (b n) -> p b n", b=TT)
        counts = small[:, 160:168]
        negc, posc = small[:, 168:176], small[:, 176:184]
        lt = small[:, 184:232]
        cmp_a = xg_mem[:, 0:64].rearrange("p (e j) -> p e j", e=E)
        cmp_b = xg_mem[:, 64:128].rearrange("p (e j) -> p e j", e=E)
        rt = hn_flat[:, KC * CAP:1024]
        flags, incl, excl = (rt[:, NFLAG * m:NFLAG * (m + 1)] for m in range(3))
        over_e, base, tabf = flags[:, 0:MAX_OVER], flags[:, MAX_OVER:2 * MAX_OVER], excl[0:1, 0:2 + MAX_OVER]
        hit = rt[:, 3 * NFLAG:(3 + MAX_OVER) * NFLAG].rearrange("p (o f) -> p o f", o=MAX_OVER)
        hit2_flat = rt[:, (3 + MAX_OVER) * NFLAG:(3 + 2 * MAX_OVER) * NFLAG]
        hit2 = hit2_flat.rearrange("p (o f) -> p o f", o=MAX_OVER)
        prod = hit2_flat[:, 0:MAX_OVER * E].rearrange("p (o e) -> p o e", o=MAX_OVER)
        onehot_at = (3 + 2 * MAX_OVER) * NFLAG
        onehot = rt[:, onehot_at:onehot_at + MAX_OVER * E].rearrange("p (o e) -> p o e", o=MAX_OVER)
        rank1 = lt[:, 0:16].rearrange("p (b e) -> p b e", b=TT)

        loaded = [sem(f"loaded{s}") for s in range(SLOTS)]
        used = sem("weights_used")
        x_in, cst_in, rows_sem, misc_in = sem("x_in"), sem("cst_in"), sem("rows_sem"), sem("misc_in")
        attn_in = sem("attn_in")
        out_sem = sem("out_sem")
        dve_chain, act_chain = sem("dve_chain"), sem("act_chain")
        x_turned, rows_turned, par_ready = sem("x_turned"), sem("rows_turned"), sem("par_ready")
        h_ready = sem("h_ready")
        sq_ready, sq_summed, rms_ready = sem("sq_ready"), sem("sq_summed"), sem("rms_ready")
        hn_ready = sem("hn_ready")
        x_proj, x_evac, conv_done = sem("x_proj"), sem("x_evac"), sem("conv_done")
        gates_ready, gates_evac, ix_done = sem("gates_ready"), sem("gates_evac"), sem("ix_done")
        lam_exp, negc_ready, decay_ready, tanh_ready, var_ready, root_ready = (
            sem(n) for n in ("lam_exp", "negc_ready", "decay_ready", "tanh_ready", "var_ready", "root_ready"))
        y_proj, gelu_done, z_ready, o_proj = sem("y_proj"), sem("gelu_done"), sem("z_ready"), sem("o_proj")
        angle_ready, sin_ready, zero_ready = sem("angle_ready"), sem("sin_ready"), sem("zero_ready")
        f_gu, f_silu, f_h, f_acc = sem("ffn_gu_ready"), sem("ffn_silu_done"), sem("ffn_h_done"), sem("ffn_acc_ready")
        kv_proj, k_raw_ready, kd_rot, kd_ready, v_ready = (
            sem(n) for n in ("kv_proj", "k_raw_ready", "kd_rot", "kd_ready", "v_ready"))
        q_proj, q_raw, q_rot, q_ready = sem("q_proj"), sem("q_raw"), sem("q_rot"), sem("q_ready")
        scores, masked, negmax, exp_done, norm_done = (
            sem(n) for n in ("scores", "masked", "negmax", "exp_done", "norm_done"))
        p_turned, p_copied, heads_ps, heads_ready, wo_proj = (
            sem(n) for n in ("p_turned", "p_copied", "heads_ps", "heads_ready", "wo_proj"))
        logits_ready, gap_ready, gap_exp, sel_ready, pos_ready, table_ready = (
            sem(n) for n in ("logits_ready", "gap_ready", "gap_exp", "sel_ready", "pos_ready", "table_ready"))
        hn_turned, hn_tok_ready = sem("hn_turned"), sem("hn_tok_ready")
        onehot_ready, weighted_ready, gathered, xg_ready = (
            sem(n) for n in ("onehot_ready", "weighted_ready", "gathered", "xg_ready"))
        hi_done, lo_done, parts_used = sem("hi_done"), sem("lo_done"), sem("parts_used")
        m_silu, m_h, h_turned, ht_hi_ready, ht_ready, xg_hi_ready, y_staged = (
            sem(n) for n in ("moe_silu_done", "moe_h_done", "h_turned", "ht_hi_ready", "ht_ready", "xg_hi_ready", "y_staged"))
        g_turned, g_ready, scattered, added = (sem(n) for n in ("g_turned", "g_ready", "scattered", "added"))
        out_turned, out_even, out_odd = sem("out_turned"), sem("out_even"), sem("out_odd")

        slot_of = list(range(LRU_LOADS)) + 6 * ORDER_FFN + ORDER_ATT
        total = {s: 0 for s in range(SLOTS)}
        arrive = []
        for k, s in enumerate(slot_of):
            total[s] += 32 if k == 4 else 16
            arrive.append(total[s])
        moe_base = dict(total)

        def columns(w, c0):
            return w[:, c0:c0 + CHF].rearrange("(k p) c -> p k c", p=P)

        def as_columns(s):
            return ring[:, s, :].rearrange("p (k c) -> p k c", k=KC)

        def as_rows(s):
            return ring[:, s, :].rearrange("p (f d) -> p f d", f=2)

        def pieces(n, lag):
            seq = []
            for c in range(n + lag):
                if c < n:
                    seq += [("gate", c), ("up", c)]
                if c >= lag:
                    seq.append(("down", c - lag))
            return seq

        FFN_PIECES, MOE_PIECES = pieces(HALF, 1), pieces(NCH, 2)
        FFN_AT = {piece: j for j, piece in enumerate(FFN_PIECES)}
        MOE_AT = {piece: j for j, piece in enumerate(MOE_PIECES)}

        block = ctx.enter_context(nc.Block())

        @block.sync
        def _(sp):
            sp.dma_start(x_tok, x[0].rearrange("(b p) d -> p b d", p=P)).then_inc(x_in, 16)
            w_in, w_out = lru_w_in[0], lru_w_out[0]
            w_qkv, w_o = attn_w_qkv[0], attn_w_o[0]
            early = [("c", w_in, D + CHF * t) for t in range(4)] + [("g", None, 0)]
            early += [("c", w_in, CHF * t) for t in range(4)] + [("c", w_out, CHF * t) for t in range(4)]

            sp.wait_ge(cst_in, 16)
            sp.wait_ge(rows_sem, 16 * 12)

            def load_early(k, kind, w, c0):
                s = slot_of[k]
                if s in slot_of[:k]:
                    before = max(j for j in range(k) if slot_of[j] == s)
                    sp.wait_ge(used, before + 1)
                if kind == "g":
                    v = ring[:, s, :].rearrange("p (m n d) -> p m n d", m=2, n=KC)
                    sp.dma_start(v[:, 0], lru_w_a[0].rearrange("n c d -> c n d")).then_inc(loaded[s], 16)
                    sp.dma_start(v[:, 1], lru_w_x[0].rearrange("n c d -> c n d")).then_inc(loaded[s], 16)
                else:
                    sp.dma_start(as_columns(s), columns(w, c0)).then_inc(loaded[s], 16)

            for k, (kind, w, c0) in enumerate(early):
                load_early(k, kind, w, c0)

            with sp.Fori(0, 2) as t:
                for j, (what, c) in enumerate(FFN_PIECES):
                    s = ORDER_FFN[j % HALF]
                    sp.wait_ge(used, 3 * HALF * t + (LRU_LOADS + j - HALF + 1))
                    if what == "down":
                        src = ffn_w_down[0].rearrange("(u f p) d -> u p f d", p=P, f=2)[t * HALF + c]
                        sp.dma_start(as_rows(s), src).then_inc(loaded[s], 16)
                    else:
                        w = (ffn_w_gate if what == "gate" else ffn_w_up)[0]
                        src = w.rearrange("(k p) (u c) -> u p k c", p=P, c=CHF)[t * HALF + c]
                        sp.dma_start(as_columns(s), src).then_inc(loaded[s], 16)

            late = [(w_qkv, D), (w_qkv, D + CHF)] + [(w_qkv, CHF * t) for t in range(4)]
            late += [(w_o, CHF * t) for t in range(4)]
            for n, (w, c0) in enumerate(late):
                load_early(FIRST_ATT + n, "c", w, c0)

            def load_item(i, e):
                for j, (what, c) in enumerate(MOE_PIECES):
                    s = ORDER_MOE[j % SLOTS]
                    if j < SLOTS:
                        sp.wait_ge(used, FIRST_MOE - SLOTS + 1 + j)
                    sp.wait_ge(lo_done, PIECES * i + (j + 1))
                    if what == "down":
                        src = moe_w_down[0].rearrange("e (u f p) d -> e u p f d", p=P, f=2)[e, c]
                        sp.dma_start(as_rows(s), src).then_inc(loaded[s], 16)
                    else:
                        w = (moe_w_gate if what == "gate" else moe_w_up)[0]
                        src = w.rearrange("e (k p) (u c) -> e u p k c", p=P, c=CHF)[e, c]
                        sp.dma_start(as_columns(s), src).then_inc(loaded[s], 16)

            with sp.Fori(0, E) as i:
                load_item(i, i)
            sp.wait_ge(table_ready, 1)
            n_over = sp.value_load(table[0:1, 0:1], min_val=0, max_val=MAX_OVER)
            with sp.Fori(0, MAX_OVER) as o:
                with sp.If(o < n_over):
                    e = sp.value_load(table[0:1, bass.ds(o + 2, 1)], min_val=0, max_val=E - 1)
                    load_item(o + E, e)

            for b in range(TT):
                sp.wait_ge(out_even, 2 * (b + 1))
                sp.wait_ge(out_odd, 2 * (b + 1))
                sp.dma_start(out[0].rearrange("(b p) d -> b p d", p=P)[b], out_tok[:, b, :]).then_inc(out_sem, 16)
            sp.wait_ge(out_sem, 16 * TT)

        @block.scalar
        def _(act):
            links = [0]

            def link(ins):
                links[0] += 1
                ins.then_inc(act_chain, 1)
                act.wait_ge(act_chain, links[0])

            act.dma_start(cst[:, :], consts).then_inc(cst_in, 16)
            srcs = [("mix0", norm_mix[0:1]), ("mix1", norm_mix[1:2]), ("ffn0", norm_ffn[0:1]),
                    ("ffn1", norm_ffn[1:2]), ("final", norm_final.rearrange("(a d) -> a d", a=1)),
                    ("conv_w", lru_conv_w[0]), ("conv_b", lru_conv_b), ("b_a", lru_b_a), ("b_x", lru_b_x),
                    ("lam", lru_lambda), ("b_qkv", attn_b_qkv), ("b_o", attn_b_o)]
            for name, src in srcs:
                a, n = ROWS[name]
                act.dma_start(rows_in[a:a + n, :], src.rearrange("a (c p) -> (a c) p", p=P)).then_inc(rows_sem, 16)
            act.dma_start(pos_i, positions.to_broadcast([P, T])).then_inc(misc_in, 16)
            with nc.allow_non_contiguous_dma(reason="the router's rows are 32 bytes long"):
                act.dma_start(wr[:, :, :], moe_w_router[0].rearrange("(k p) e -> p k e", p=P)).then_inc(misc_in, 16)

            def squares(n):
                for c in range(KC):
                    act.wait_ge(h_ready, KC * n + c + 1)
                    if KC * n + c >= 2:
                        act.wait_ge(sq_summed, KC * n + c - 1)
                    nc.scalar.activation(sq[:, c % 2], h[:, c], ACT.Square).then_inc(sq_ready, 1)

            def root(n, bank):
                act.wait_ge(sq_summed, KC * (n + 1))
                nc.scalar.activation(rstd, ps[:, bank, 0:T], ACT.Sqrt, bias=eps_col, scale=1.0 / D).then_inc(rms_ready, 1)

            eps_col = lt[:, 47:48]
            act.wait_ge(lam_exp, 1)
            nc.scalar.activation(lt[:, 8:16], lt[:, 0:8], ACT.Exp, scale=-1.0).then_inc(lam_exp, 1)
            act.wait_ge(angle_ready, 1)
            nc.scalar.activation(cosv, ang2, ACT.Sin).then_inc(sin_ready, 1)
            nc.scalar.activation(sinv, ang, ACT.Sin).then_inc(sin_ready, 1)
            squares(0)
            root(0, 7)

            for t in range(KC):
                act.wait_ge(x_proj, t + 1)
                if t >= 2:
                    act.wait_ge(conv_done, t - 1)
                nc.scalar.copy(xpad[:, t % 2, 3:3 + T], ps[:, t % 4, 0:T]).then_inc(x_evac, 1)
            for t in range(KC):
                act.wait_ge(gates_ready, t + 1)
                if t >= 2:
                    act.wait_ge(ix_done, t - 1)
                nc.scalar.activation(rr[:, t], ps[:, 4 + t % 2, 0:T], ACT.Sigmoid, bias=param("b_a", t)).then_inc(gates_evac, 1)
                nc.scalar.activation(igate[:, t % 2], ps[:, 4 + t % 2, T:2 * T], ACT.Sigmoid,
                                     bias=param("b_x", t)).then_inc(gates_evac, 1)
            act.wait_ge(negc_ready, 1)
            act.wait_ge(gates_evac, 2 * KC)
            for t in range(KC):
                nc.scalar.activation(aa[:, t], rr[:, t], ACT.Exp, scale=negc[:, t:t + 1]).then_inc(decay_ready, 1)
            act.wait_ge(decay_ready, KC)
            for t in range(KC):
                nc.scalar.activation(rr[:, t], rr[:, t], ACT.Tanh, scale=posc[:, t:t + 1]).then_inc(tanh_ready, 1)
            for t in range(KC):
                act.wait_ge(var_ready, t + 1)
                nc.scalar.activation(rr[:, t], rr[:, t], ACT.Sqrt).then_inc(root_ready, 1)
            for t in range(KC):
                act.wait_ge(y_proj, t + 1)
                nc.scalar.activation(yy[:, t], ps[:, t % 4, 0:T], ACT.Gelu_apprx_tanh).then_inc(gelu_done, 1)
            squares(1)
            root(1, 7)

            with act.Fori(0, 2) as t:
                for c in range(HALF):
                    for f in range(2):
                        act.wait_ge(f_gu, 2 * HALF * t + (2 * c + f + 1))
                        nc.scalar.activation(ffn_h[:, c % 2, f], ps[:, 2 * (c % 2) + f, 0:T], ACT.Silu).then_inc(f_silu, 1)
            squares(2)
            root(2, 0)

            act.wait_ge(hn_ready, 3 * KC)
            act.dma_start(sinks, attn_sinks.to_broadcast([P, NH])).then_inc(attn_in, 16)
            act.dma_start(bv_row, attn_b_qkv[:, D + NKV * HD:]).then_inc(attn_in, 16)
            for j in range(2):
                act.wait_ge(kv_proj, j + 1)
                nc.scalar.activation(k_raw[:, j], ps[:, j, 0:T], ACT.Identity, bias=param("b_qkv", 8 + j)).then_inc(k_raw_ready, 1)
            for b in range(TT):
                act.wait_ge(kv_proj, 3 + b)
                nc.scalar.copy(v_tok[:, b], ps[:, 2 + b, 0:T]).then_inc(v_ready, 1)

            def bias_q(t):
                act.wait_ge(q_proj, t + 1)
                nc.scalar.activation(q[:, t], ps[:, t % 2, 0:T], ACT.Identity, bias=param("b_qkv", t)).then_inc(q_raw, 1)

            def soften(hd):
                act.wait_ge(negmax, hd + 1)
                st = stat[:, 16 * (hd % 3):16 * (hd % 3) + 16]
                pr = probs[:, hd % 3]
                nc.scalar.activation(pr[:, 0:P], pr[:, 0:P], ACT.Exp, bias=st[:, 4:5], accum_out=st[:, 6:7]).then_inc(exp_done, 1)
                nc.scalar.activation(pr[:, P:3 * P], pr[:, P:3 * P], ACT.Exp, bias=st[:, 5:6], accum_out=st[:, 7:8]).then_inc(exp_done, 1)
                nc.scalar.activation(st[:, 8:10], st[:, 4:6], ACT.Exp, bias=sinks[:, hd:hd + 1]).then_inc(exp_done, 1)

            def copy_probs(hd):
                act.wait_ge(p_turned, hd + 1)
                nc.scalar.copy(probs_t[:, hd % 2], ps[:, 4 + hd % 2, 0:3 * P]).then_inc(p_copied, 1)

            bias_q(0)
            for t in range(KC + 1):
                if t + 1 < KC:
                    bias_q(t + 1)
                if t < KC:
                    soften(2 * t)
                    soften(2 * t + 1)
                if t >= 1:
                    for hd in (2 * t - 2, 2 * t - 1):
                        copy_probs(hd)
                    act.wait_ge(heads_ps, t)
                    nc.scalar.copy(heads[:, t - 1], ps[:, 6, 0:T]).then_inc(heads_ready, 1)
            squares(3)
            root(3, 7)
            act.wait_ge(gap_ready, 1)
            nc.scalar.activation(gate[:, 0:2], gate[:, 0:2], ACT.Exp).then_inc(gap_exp, 1)
            for g in range(4):
                act.wait_ge(hn_turned, g + 1)
                nc.scalar.copy(hn_tok[:, g // 2, (g % 2) * 512:(g % 2) * 512 + 512], ps[:, 2 + g, :]).then_inc(hn_tok_ready, 1)

            def split(i, n):
                s = ORDER_MOE[n % SLOTS]
                act.wait_ge(loaded[s], 48 * i + (moe_base[s] + 16 * (n // SLOTS + 1)))
                act.wait_ge(parts_used, PIECES * i + (n + 1))
                nc.scalar.copy(w_hi[:, n % PARTS], ring[:, s]).then_inc(hi_done, 1)

            def weights_back(i):
                act.wait_ge(g_turned, i + 1)
                nc.scalar.copy(gt, ps[0:CAP, 4, 0:T]).then_inc(g_ready, 1)

            def item(i):
                for g in range(2):
                    act.wait_ge(gathered, 2 * i + (g + 1))
                    nc.scalar.copy(xg_hi[:, 4 * g:4 * g + 4], ps[:, 4 + g, 0:4 * CAP].rearrange("p (c n) -> p c n", c=4)).then_inc(xg_hi_ready, 1)
                for c in range(NCH + 2):
                    if c < NCH:
                        split(i, MOE_AT[("gate", c)])
                        split(i, MOE_AT[("up", c)])
                    if c == 1:
                        weights_back(i)
                    if 1 <= c <= NCH:
                        act.wait_ge(parts_used, PIECES * i + (PARTS + MOE_AT[("up", c - 1)] + 1))
                        nc.scalar.activation(h_tok[:, (c - 1) % 2], ps[0:CAP, (c - 1) % 2, 0:CHF], ACT.Silu).then_inc(m_silu, 1)
                    if c >= 2:
                        act.wait_ge(h_turned, NCH * i + (c - 1))
                        nc.scalar.copy(ht_hi[:, c % 2], ps[:, 6 + c % 2, 0:2 * CAP].rearrange("p (f n) -> p f n", f=2)).then_inc(ht_hi_ready, 1)
                        split(i, MOE_AT[("down", c - 2)])
                act.wait_ge(parts_used, PIECES * i + (PARTS + PIECES))
                nc.scalar.copy(y_tok[:, 0:512], ps[0:CAP, 2, :]).then_inc(y_staged, 1)

            with act.Fori(0, E) as i:
                item(i)
            act.wait_ge(table_ready, 1)
            n_over = act.value_load(table[0:1, 0:1], min_val=0, max_val=MAX_OVER)
            with act.Fori(0, MAX_OVER) as o:
                with act.If(o < n_over):
                    item(o + E)
            weights_back(n_over + E)
            squares(4)
            root(4, 0)
            for g in range(1, 8, 2):
                act.wait_ge(out_turned, g + 1)
                nc.scalar.copy(out_tok[:, g // 4, (g % 4) * 256:(g % 4) * 256 + 256], ps[:, g, 0:256]).then_inc(out_odd, 1)

        @block.vector
        def _(dve):
            links = [0]

            def link(ins):
                links[0] += 1
                ins.then_inc(dve_chain, 1)
                dve.wait_ge(dve_chain, links[0])

            V = nc.vector
            V.memset(zero[:, :], 0.0).then_inc(zero_ready, 1)
            for b in range(2):
                V.memset(xpad[:, b, 0:3], 0.0).then_inc(zero_ready, 1)
            V.memset(small[:, 160:161], 0.0).then_inc(lo_done, SLOTS)
            V.memset(small[:, 96:160], 0.0).then_inc(zero_ready, 1)
            dve.wait_ge(rows_turned, 1)
            link(V.tensor_copy(par[:, :], ps[:, 4, 0:NROWS]))
            par_ready_inc = V.memset(lt[:, 47:48], EPS)
            link(par_ready_inc)
            a, n = ROWS["lam"]
            lam = par[:, a:a + n]
            link(V.tensor_scalar(lt[:, 16:24], lam, -1.0, None, ALU.mult))
            V.tensor_tensor(lt[:, 0:8], lam, lt[:, 16:24], ALU.max).then_inc(lam_exp, 1)
            dve.wait_ge(cst_in, 16)
            dve.wait_ge(misc_in, 32)
            link(V.tensor_copy(ang, pos_i))
            link(V.tensor_scalar(ang, ang, const("inv_freq"), None, ALU.mult))
            magic = 1.5 * 2.0 ** 23
            rest, parts = 2 * np.pi, []
            for _ in range(3):
                unit = 2.0 ** (np.floor(np.log2(rest)) - 7)
                parts.append(float(np.floor(rest / unit) * unit))
                rest -= parts[-1]
            parts.append(float(rest))
            link(V.tensor_scalar(turns, ang, 1.0 / (2 * np.pi), None, ALU.mult))
            link(V.tensor_scalar(turns2, turns, 0.25, magic, ALU.add, ALU.add))
            link(V.tensor_scalar(turns, turns, magic, None, ALU.add))
            link(V.tensor_scalar(turns2, turns2, -magic, None, ALU.add))
            link(V.tensor_scalar(turns, turns, -magic, None, ALU.add))
            link(V.scalar_tensor_tensor(out=ang2, in0=turns2, scalar=-parts[0], in1=ang, op0=ALU.mult, op1=ALU.add))
            link(V.scalar_tensor_tensor(out=ang, in0=turns, scalar=-parts[0], in1=ang, op0=ALU.mult, op1=ALU.add))
            for part in parts[1:]:
                link(V.scalar_tensor_tensor(out=ang2, in0=turns2, scalar=-part, in1=ang2, op0=ALU.mult, op1=ALU.add))
                link(V.scalar_tensor_tensor(out=ang, in0=turns, scalar=-part, in1=ang, op0=ALU.mult, op1=ALU.add))
            pi = float(np.nextafter(np.float32(np.pi), np.float32(0)))
            link(V.tensor_scalar(ang2, ang2, np.pi / 2, pi, ALU.add, ALU.min))
            link(V.tensor_scalar(ang2, ang2, -pi, None, ALU.max))
            V.tensor_scalar(ang, ang, pi, -pi, ALU.min, ALU.max).then_inc(angle_ready, 1)
            for c in range(KC):
                dve.wait_ge(x_turned, c // 2 + 1)
                V.tensor_copy(h[:, c], ps[:, c // 2, (c % 2) * T:(c % 2) * T + T]).then_inc(h_ready, 1)
            dve.wait_ge(lam_exp, 2)
            w, u, u2, s_ = lt[:, 8:16], lt[:, 24:32], lt[:, 32:40], negc
            link(V.tensor_scalar(u, w, 2.0, None, ALU.add))
            link(V.reciprocal(u2, u))
            link(V.tensor_tensor(u, w, u2, ALU.mult))
            link(V.tensor_tensor(u2, u, u, ALU.mult))
            link(V.memset(s_, 1.0 / 17))
            for m in range(15, 0, -2):
                link(V.tensor_tensor(s_, s_, u2, ALU.mult))
                link(V.tensor_scalar(s_, s_, 1.0 / m, None, ALU.add))
            link(V.tensor_tensor(s_, s_, u, ALU.mult))
            link(V.tensor_scalar(s_, s_, 2.0, None, ALU.mult))
            link(V.tensor_scalar(lt[:, 16:24], lt[:, 16:24], 0.0, None, ALU.max))
            link(V.tensor_tensor(s_, s_, lt[:, 16:24], ALU.add))
            link(V.tensor_scalar(posc, s_, 8.0, None, ALU.mult))
            V.tensor_scalar(negc, s_, -8.0, None, ALU.mult).then_inc(negc_ready, 1)

            def normed(n, weight):
                dve.wait_ge(rms_ready, n + 1)
                link(V.reciprocal(rstd, rstd))
                for c in range(KC):
                    V.scalar_tensor_tensor(out=hn[:, c], in0=h[:, c], scalar=param(weight, c), in1=rstd,
                                           op0=ALU.mult, op1=ALU.mult).then_inc(hn_ready, 1)

            normed(0, "mix0")
            dve.wait_ge(zero_ready, 4)
            for t in range(KC):
                dve.wait_ge(x_evac, t + 1)
                xp = xpad[:, t % 2]
                link(V.tensor_scalar(xc[:, t], xp[:, 0:T], param("conv_w", t), param("conv_b", t), ALU.mult, ALU.add))
                for k in range(1, CONV):
                    ins = V.scalar_tensor_tensor(out=xc[:, t], in0=xp[:, k:k + T], scalar=param("conv_w", KC * k + t),
                                                 in1=xc[:, t], op0=ALU.mult, op1=ALU.add)
                    if k < CONV - 1:
                        link(ins)
                    else:
                        ins.then_inc(conv_done, 1)
            dve.wait_ge(conv_done, KC)
            for t in range(KC):
                dve.wait_ge(gates_evac, 2 * t + 2)
                V.tensor_tensor(xc[:, t], igate[:, t % 2], xc[:, t], ALU.mult).then_inc(ix_done, 1)
            for t in range(KC):
                dve.wait_ge(tanh_ready, t + 1)
                link(V.tensor_tensor(asq[:, t % 2], aa[:, t], aa[:, t], ALU.mult))
                V.scalar_tensor_tensor(out=rr[:, t], in0=asq[:, t % 2], scalar=1.0, in1=rr[:, t],
                                       op0=ALU.add, op1=ALU.mult).then_inc(var_ready, 1)
            dve.wait_ge(ix_done, KC)
            for t in range(KC):
                dve.wait_ge(root_ready, t + 1)
                link(V.tensor_tensor(xc[:, t], rr[:, t], xc[:, t], ALU.mult))
                link(V.tensor_tensor_scan(rr[:, t], aa[:, t], xc[:, t], 0.0, ALU.mult, ALU.add))
                dve.wait_ge(gelu_done, t + 1)
                V.tensor_tensor(yy[:, t], rr[:, t], yy[:, t], ALU.mult).then_inc(z_ready, 1)
            for c in range(KC):
                dve.wait_ge(o_proj, c + 1)
                V.tensor_tensor(h[:, c], ps[:, c % 4, 0:T], h[:, c], ALU.add).then_inc(h_ready, 1)
            dve.wait_ge(h_ready, 2 * KC)
            normed(1, "ffn0")
            with dve.Fori(0, 2) as t:
                for c in range(HALF):
                    for f in range(2):
                        dve.wait_ge(f_silu, 2 * HALF * t + (2 * c + f + 1))
                        hh = ffn_h[:, c % 2, f]
                        V.tensor_tensor(hh, ps[:, 2 * (c % 2) + f, T:2 * T], hh, ALU.mult).then_inc(f_h, 1)
            for c in range(KC):
                dve.wait_ge(f_acc, c // 2 + 1)
                V.tensor_tensor(h[:, c], ps[:, 4 + c // 2, (c % 2) * T:(c % 2) * T + T], h[:, c], ALU.add).then_inc(h_ready, 1)
            dve.wait_ge(h_ready, 3 * KC)
            normed(2, "mix1")
            dve.wait_ge(sin_ready, 2)
            for g in range(NKV):
                dve.wait_ge(kd_rot, g + 1)
                link(V.tensor_tensor(rope_a[:, g % 2], ps[:, 4 + g, T:2 * T], sinv, ALU.mult))
                link(V.tensor_tensor(kd[:, g], ps[:, 4 + g, 0:T], cosv, ALU.mult))
                V.tensor_tensor(kd[:, g], kd[:, g], rope_a[:, g % 2], ALU.add).then_inc(kd_ready, 1)
            dve.wait_ge(kd_ready, NKV)

            def rope_q(t):
                dve.wait_ge(q_rot, t + 1)
                link(V.tensor_tensor(rope_a[:, t % 2], ps[:, 2 + t % 2, 0:T], sinv, ALU.mult))
                link(V.tensor_tensor(q[:, t], q[:, t], cosv, ALU.mult))
                ins = V.tensor_tensor(q[:, t], q[:, t], rope_a[:, t % 2], ALU.add)
                ins.then_inc(q_ready, 1)

            def row_max(hd):
                dve.wait_ge(scores, hd + 1)
                if hd >= 3:
                    dve.wait_ge(p_turned, hd - 2)
                st = stat[:, 16 * (hd % 3):16 * (hd % 3) + 16]
                pr = probs[:, hd % 3]
                link(V.scalar_tensor_tensor(out=pr, in0=ps[:, SCORE_BANK[hd % 2], 0:3 * P], scalar=HD ** -0.5,
                                            in1=const("mask"), op0=ALU.mult, op1=ALU.add))
                V.tensor_reduce(st[:, 0:1], pr[:, 0:P], AX.X, ALU.max)
                link(V.tensor_reduce(st[:, 1:2], pr[:, P:3 * P], AX.X, ALU.max))
                V.tensor_scalar(st[:, 4:6], st[:, 0:2], sinks[:, hd:hd + 1], -1.0, ALU.max, ALU.mult).then_inc(negmax, 1)

            def normalise(hd):
                dve.wait_ge(exp_done, 3 * hd + 3)
                st = stat[:, 16 * (hd % 3):16 * (hd % 3) + 16]
                pr = probs[:, hd % 3]
                link(V.tensor_tensor(st[:, 10:12], st[:, 6:8], st[:, 8:10], ALU.add))
                link(V.reciprocal(st[:, 12:14], st[:, 10:12]))
                link(V.tensor_scalar(pr[:, 0:P], pr[:, 0:P], st[:, 12:13], None, ALU.mult))
                V.tensor_scalar(pr[:, P:3 * P], pr[:, P:3 * P], st[:, 13:14], None, ALU.mult).then_inc(norm_done, 1)

            SCORE_BANK = (7, 3)
            dve.wait_ge(attn_in, 32)
            rope_q(0)
            for t in range(KC):
                row_max(2 * t)
                row_max(2 * t + 1)
                if t + 1 < KC:
                    rope_q(t + 1)
                normalise(2 * t)
                normalise(2 * t + 1)
            for c in range(KC):
                dve.wait_ge(wo_proj, c + 1)
                V.scalar_tensor_tensor(out=h[:, c], in0=ps[:, c % 4, 0:T], scalar=param("b_o", c), in1=h[:, c],
                                       op0=ALU.add, op1=ALU.add).then_inc(h_ready, 1)
            dve.wait_ge(h_ready, 4 * KC)
            normed(3, "ffn1")

            dve.wait_ge(logits_ready, 1)
            link(V.tensor_copy(logit, ps[:, 0, 0:16].rearrange("p (b e) -> p b e", b=TT)))
            for b in range(TT):
                link(V.max(top[:, b], logit[:, b]))
                V.tensor_tensor(gate[:, b:b + 1], top[:, b, 1:2], top[:, b, 0:1], ALU.subtract).then_inc(gap_ready if b else dve_chain, 1)
                if not b:
                    links[0] += 1
            for b in range(TT):
                each = logit[:, b].unsqueeze(1).to_broadcast([P, E, E])
                own = logit[:, b].unsqueeze(2).to_broadcast([P, E, E])
                V.tensor_tensor(cmp_a, each, own, ALU.is_gt).then_inc(dve_chain, 1)
                link(V.tensor_tensor(cmp_b, each, own, ALU.is_equal))
                links[0] += 1
                dve.wait_ge(dve_chain, links[0])
                link(V.tensor_tensor(cmp_b, cmp_b, const("earlier").rearrange("p (e j) -> p e j", e=E), ALU.mult))
                link(V.tensor_tensor(cmp_a, cmp_a, cmp_b, ALU.add))
                link(V.tensor_reduce(order[:, b], cmp_a, AX.X, ALU.add))
            V.tensor_scalar(chosen, order, float(TOPK), None, ALU.is_lt).then_inc(sel_ready, 1)
            dve.wait_ge(gap_exp, 1)
            link(V.tensor_scalar(gate[:, 2:4], gate[:, 0:2], 1.0, None, ALU.add))
            link(V.reciprocal(gate[:, 4:6], gate[:, 2:4]))
            link(V.tensor_tensor(gate[:, 6:8], gate[:, 4:6], gate[:, 0:2], ALU.mult))
            for b in range(TT):
                link(V.tensor_scalar(w2nd[:, b], order[:, b], 1.0, gate[:, 6 + b:7 + b], ALU.is_equal, ALU.mult))
                link(V.tensor_scalar(comb[:, b, 1:1 + E], order[:, b], 0.0, gate[:, 4 + b:5 + b], ALU.is_equal, ALU.mult))
                link(V.tensor_tensor(comb[:, b, 1:1 + E], comb[:, b, 1:1 + E], w2nd[:, b], ALU.add))
            dve.wait_ge(pos_ready, 1)
            link(V.scalar_tensor_tensor(out=rank1, in0=ps[:, 1, 0:16].rearrange("p (b e) -> p b e", b=TT), scalar=1.0,
                                        in1=chosen, op0=ALU.add, op1=ALU.mult))
            link(V.tensor_copy(counts, ps[:, 1, 16:24]))
            link(V.tensor_scalar(rank[:, :, 0:1], rank[:, :, 0:1], -1.0, None, ALU.add))
            link(V.tensor_scalar(rank[:, :, NCOL - 1:NCOL], rank[:, :, NCOL - 1:NCOL], -1.0, None, ALU.add))
            link(V.tensor_scalar(rank[:, :, 1:1 + E], rank1, -1.0, None, ALU.add))
            for b in range(TT):
                V.tensor_scalar(sel[:, b], const("iota"), rank[:, b, 1:2], None, ALU.is_equal).then_inc(onehot_ready, 1)
                V.tensor_scalar(selw[:, b], const("iota"), rank[:, b, 0:1], comb[:, b, 0:1], ALU.is_equal, ALU.mult).then_inc(weighted_ready, 1)
            dve.wait_ge(hn_turned, 4)
            V.memset(y_tok, 0.0).then_inc(y_staged, 1)
            many = counts.unsqueeze(2).to_broadcast([P, E, TILES_MORE])
            f3 = flags.rearrange("p (e t) -> p e t", e=E)
            link(V.tensor_tensor(f3, many, const("thr").rearrange("p (e t) -> p e t", e=E), ALU.is_gt))
            link(V.tensor_tensor_scan(incl, const("ones")[:, 0:NFLAG], flags, 0.0, ALU.mult, ALU.add))
            link(V.tensor_tensor(excl, incl, flags, ALU.subtract))
            shape = [P, MAX_OVER, NFLAG]
            link(V.tensor_tensor(hit, excl.unsqueeze(1).to_broadcast(shape), const("iota_over").unsqueeze(2).to_broadcast(shape), ALU.is_equal))
            link(V.tensor_tensor(hit, hit, flags.unsqueeze(1).to_broadcast(shape), ALU.mult))
            link(V.tensor_tensor(hit2, hit, const("flag_e").unsqueeze(1).to_broadcast(shape), ALU.mult))
            link(V.tensor_reduce(over_e, hit2, AX.X, ALU.add))
            link(V.tensor_tensor(hit2, hit, const("thr").unsqueeze(1).to_broadcast(shape), ALU.mult))
            link(V.tensor_reduce(base, hit2, AX.X, ALU.add))
            link(V.tensor_reduce(onehot, hit.rearrange("p o (e t) -> p o e t", e=E), AX.X, ALU.add))
            oe = [P, MAX_OVER, E]
            for b in range(TT):
                link(V.tensor_tensor(prod, onehot, rank1[:, b].unsqueeze(1).to_broadcast(oe), ALU.mult))
                link(V.tensor_reduce(rank[:, b, 1 + E:1 + E + MAX_OVER], prod, AX.X, ALU.add))
                link(V.scalar_tensor_tensor(out=rank[:, b, 1 + E:1 + E + MAX_OVER], in0=rank[:, b, 1 + E:1 + E + MAX_OVER],
                                            scalar=-1.0, in1=base, op0=ALU.add, op1=ALU.subtract))
                link(V.tensor_tensor(prod, onehot, comb[:, b, 1:1 + E].unsqueeze(1).to_broadcast(oe), ALU.mult))
                link(V.tensor_reduce(comb[:, b, 1 + E:1 + E + MAX_OVER], prod, AX.X, ALU.add))
            link(V.tensor_copy(tabf[:, 0:1], incl[0:1, NFLAG - 1:NFLAG]))
            link(V.tensor_copy(tabf[:, 1:2], incl[0:1, NFLAG - 1:NFLAG]))
            link(V.tensor_copy(tabf[:, 2:2 + MAX_OVER], over_e[0:1, :]))
            link(V.tensor_copy(table[:, :], tabf))
            V.memset(h_tok[:, 0, 0:1], 0.0).then_inc(table_ready, 1)

            SCATTER_BANK = (5, 4, 5, 4)

            def add_back(i, m):
                dve.wait_ge(scattered, 4 * i + (m + 1))
                hh = h[:, 2 * m:2 * m + 2, :].rearrange("p c t -> p (c t)")
                return V.tensor_tensor(hh, ps[:, SCATTER_BANK[m], :], hh, ALU.add).then_inc(added, 1)

            def split(i, n):
                dve.wait_ge(hi_done, PIECES * i + (n + 1))
                V.tensor_tensor(w_lo[:, n % PARTS], ring[:, ORDER_MOE[n % SLOTS]], w_hi[:, n % PARTS].bitcast(F32),
                                ALU.subtract).then_inc(lo_done, 1)

            def item(i):
                for g in range(2):
                    dve.wait_ge(xg_hi_ready, 2 * i + (g + 1))
                    V.tensor_tensor(xg_lo[:, 4 * g:4 * g + 4], ps[:, 4 + g, 0:4 * CAP].rearrange("p (c n) -> p c n", c=4),
                                    xg_hi[:, 4 * g:4 * g + 4].bitcast(F32), ALU.subtract).then_inc(xg_ready, 1)
                for c in range(NCH + 2):
                    if c < NCH:
                        split(i, MOE_AT[("gate", c)])
                        split(i, MOE_AT[("up", c)])
                    if 1 <= c <= NCH:
                        dve.wait_ge(m_silu, NCH * i + c)
                        hh = h_tok[:, (c - 1) % 2]
                        V.tensor_tensor(hh, ps[0:CAP, (c - 1) % 2, CHF:2 * CHF], hh, ALU.mult).then_inc(m_h, 1)
                    if c >= 2:
                        dve.wait_ge(ht_hi_ready, NCH * i + (c - 1))
                        V.tensor_tensor(ht_lo[:, c % 2], ps[:, 6 + c % 2, 0:2 * CAP].rearrange("p (f n) -> p f n", f=2),
                                        ht_hi[:, c % 2].bitcast(F32), ALU.subtract).then_inc(ht_ready, 1)
                        split(i, MOE_AT[("down", c - 2)])
                    if c in (4, 6):
                        add_back(i, c - 4)
                        add_back(i, c - 3)
                    if c == 8:
                        for b in range(TT):
                            V.tensor_scalar(selw[:, b], const("iota"), rank[:, b, bass.ds(i + 1, 1)],
                                            comb[:, b, bass.ds(i + 1, 1)], ALU.is_equal, ALU.mult).then_inc(weighted_ready, 1)
                            V.tensor_scalar(sel[:, b], const("iota"), rank[:, b, bass.ds(i + 2, 1)], None,
                                            ALU.is_equal).then_inc(onehot_ready, 1)
                dve.wait_ge(parts_used, PIECES * i + (PARTS + PIECES))
                V.tensor_copy(y_tok[:, 512:1024], ps[0:CAP, 3, :]).then_inc(y_staged, 1)

            with dve.Fori(0, E) as i:
                item(i)
            n_over = dve.value_load(table[0:1, 0:1], min_val=0, max_val=MAX_OVER)
            with dve.Fori(0, MAX_OVER) as o:
                with dve.If(o < n_over):
                    item(o + E)
            last = n_over + E
            for m in range(4):
                add_back(last, m)
            dve.wait_ge(added, 4 * last + 4)
            V.memset(small[:, 160:161], 0.0).then_inc(h_ready, KC)
            normed(4, "final")
            for g in range(0, 8, 2):
                dve.wait_ge(out_turned, g + 1)
                V.tensor_copy(out_tok[:, g // 4, (g % 4) * 256:(g % 4) * 256 + 256], ps[:, g, 0:256]).then_inc(out_even, 1)

        @block.tensor
        def _(pe):
            ident = const("ident")

            def arrived(k):
                pe.wait_ge(loaded[slot_of[k]], arrive[k])

            def sum_square(n, c, bank):
                pe.wait_ge(sq_ready, KC * n + c + 1)
                mm = nc.tensor.matmul(ps[:, bank, 0:T], const("ones"), sq[:, c % 2], start=(c == 0), stop=(c == KC - 1))
                mm.then_inc(sq_summed, 1)

            def tile(bank, w, col, rhs, waits=None, c0=0, frees=False):
                for k in range(KC):
                    if waits:
                        waits(k)
                    mm = nc.tensor.matmul(ps[:, bank, c0:c0 + T], w[:, k, col:col + P], rhs[:, k], start=(k == 0), stop=(k == KC - 1))
                    if frees and k == 0:
                        mm.then_inc(used, 1)
                return mm

            pe.wait_ge(cst_in, 16)
            pe.wait_ge(rows_sem, 16 * 12)
            nc.tensor.transpose(ps[:, 4, 0:NROWS], rows_in, cst[0:NROWS, 0:NROWS]).then_inc(rows_turned, 1)
            pe.wait_ge(x_in, 16)
            for c in range(KC):
                for b in range(TT):
                    col = (c % 2) * T + b * P
                    mm = nc.tensor.transpose(ps[:, c // 2, col:col + P], x_tok[:, b, c * P:(c + 1) * P], ident)
                if c % 2:
                    mm.then_inc(x_turned, 1)
            for c in range(KC):
                sum_square(0, c, 7)

            for t in range(KC):
                arrived(t // 2)
                if t >= 4:
                    pe.wait_ge(x_evac, t - 3)
                mm = tile(t % 4, as_columns(slot_of[t // 2]), (t % 2) * P, hn,
                          (lambda k: pe.wait_ge(hn_ready, k + 1)) if t == 0 else None, frees=t in (2, 4, 6))
                mm.then_inc(x_proj, 1)
            arrived(4)
            wg = ring[:, slot_of[4], :].rearrange("p (m n d) -> p m n d", m=2, n=KC)
            for t in range(KC):
                pe.wait_ge(conv_done, t + 1)
                if t >= 2:
                    pe.wait_ge(gates_evac, 2 * (t - 1))
                for m in range(2):
                    mm = nc.tensor.matmul(ps[:, 4 + t % 2, m * T:(m + 1) * T], wg[:, m, t], xc[:, t], start=True, stop=True)
                    if t == 0 and m == 0:
                        mm.then_inc(used, 1)
                mm.then_inc(gates_ready, 1)
            pe.wait_ge(x_evac, KC)
            for t in range(KC):
                arrived(5 + t // 2)
                if t >= 4:
                    pe.wait_ge(gelu_done, t - 3)
                mm = tile(t % 4, as_columns(slot_of[5 + t // 2]), (t % 2) * P, hn, frees=t % 2 == 0)
                mm.then_inc(y_proj, 1)
            for t in range(KC):
                arrived(9 + t // 2)
                if t >= 4:
                    pe.wait_ge(h_ready, KC + t - 3)
                else:
                    pe.wait_ge(gelu_done, t + 5)
                mm = tile(t % 4, as_columns(slot_of[9 + t // 2]), (t % 2) * P, yy,
                          (lambda k: pe.wait_ge(z_ready, k + 1)) if t == 0 else None, frees=t % 2 == 0)
                mm.then_inc(o_proj, 1)
                if t >= 1:
                    sum_square(1, t - 1, 7)
            sum_square(1, KC - 1, 7)

            def open_banks(banks):
                pe.wait_ge(zero_ready, 1)
                for b in banks:
                    mm = nc.tensor.matmul(ps[:, b, :], zero[:, 0:P], zero[:, :], start=True, stop=True)
                mm.then_inc(used, 1)

            pe.wait_ge(rms_ready, 2)
            open_banks(range(4, 8))
            pe.wait_ge(hn_ready, 2 * KC)

            with pe.Fori(0, 2) as t:
                def ffn_arrived(piece):
                    j = FFN_AT[piece]
                    s = ORDER_FFN[j % HALF]
                    pe.wait_ge(loaded[s], 48 * t + arrive[LRU_LOADS + j])
                    return s

                def ffn_down(c):
                    s = ffn_arrived(("down", c))
                    for f in range(2):
                        pe.wait_ge(f_h, 2 * HALF * t + (2 * c + f + 1))
                        for d in range(KC):
                            mm = nc.tensor.matmul(ps[:, 4 + d // 2, (d % 2) * T:(d % 2 + 1) * T], as_rows(s)[:, f, d * P:(d + 1) * P],
                                                  ffn_h[:, c % 2, f], start=False, stop=False, skip_group_check=True)
                            if f == 0 and d == 0 and c < HALF - 1:
                                mm.then_inc(used, 1)
                    mm.then_inc(used, 1)

                for c in range(HALF):
                    slots = [ffn_arrived((m, c)) for m in ("gate", "up")]
                    for f in range(2):
                        for m in range(2):
                            mm = tile(2 * (c % 2) + f, as_columns(slots[m]), f * P, hn, c0=m * T, frees=(c, f, m) == (1, 0, 0))
                            if f == 1 and m == 0:
                                mm.then_inc(used, 1)
                        mm.then_inc(f_gu, 1)
                    if c:
                        ffn_down(c - 1)
                ffn_down(HALF - 1)
            for b in range(4, 8):
                nc.tensor.matmul(ps[:, b, :], zero[:, 0:P], zero[:, :], start=False, stop=True, skip_group_check=True).then_inc(f_acc, 1)
            for c in range(KC):
                sum_square(2, c, 0)

            pe.wait_ge(rms_ready, 3)
            pe.wait_ge(hn_ready, 3 * KC)
            arrived(FIRST_ATT)
            wk = as_columns(slot_of[FIRST_ATT])
            for j in range(2):
                mm = tile(j, wk, j * P, hn)
                mm.then_inc(kv_proj, 1)
            arrived(FIRST_ATT + 1)
            wv = as_columns(slot_of[FIRST_ATT + 1])
            pe.wait_ge(attn_in, 32)
            for b in range(TT):
                mm = nc.tensor.matmul(ps[:, 2 + b, 0:T], const("ones", 1), bv_row, start=True, stop=False)
                if b == 0:
                    mm.then_inc(used, 1)
                for k in range(KC):
                    mm = nc.tensor.matmul(ps[:, 2 + b, 0:T], hn[:, k, b * P:(b + 1) * P], wv[:, k, :], start=False, stop=(k == KC - 1))
                mm.then_inc(kv_proj, 1)
            pe.wait_ge(k_raw_ready, 2)
            for g in range(NKV):
                mm = nc.tensor.matmul(ps[:, 4 + g, 0:T], const(f"dup{g % 2}"), k_raw[:, g // 2], start=True, stop=True)
                if g == 0:
                    mm.then_inc(used, 1)
                nc.tensor.matmul(ps[:, 4 + g, T:2 * T], const(f"rotdup{g % 2}"), k_raw[:, g // 2], start=True, stop=True).then_inc(kd_rot, 1)
            pe.wait_ge(v_ready, 2)

            SCORE_BANK = (7, 3)

            def project_q(t):
                arrived(FIRST_ATT + 2 + t // 2)
                if t >= 2:
                    pe.wait_ge(q_raw, t - 1)
                mm = tile(t % 2, as_columns(slot_of[FIRST_ATT + 2 + t // 2]), (t % 2) * P, hn, frees=t in (2, 4, 6))
                mm.then_inc(q_proj, 1)

            def rotate_q(t):
                pe.wait_ge(q_raw, t + 1)
                if t >= 1:
                    pe.wait_ge(negmax, 2 * t)
                nc.tensor.matmul(ps[:, 2 + t % 2, 0:T], const("rot"), q[:, t], start=True, stop=True).then_inc(q_rot, 1)

            def score(hd):
                pe.wait_ge(q_ready, hd // 2 + 1)
                if hd >= 2:
                    pe.wait_ge(negmax, hd - 1)
                o, t, g = (hd % 2) * HD, hd // 2, hd // GROUP
                bank = SCORE_BANK[hd % 2]
                mm = nc.tensor.matmul(ps[:, bank, 0:P], q[o:o + HD, t, 0:P], kd[o:o + HD, g, 0:P], start=True, stop=True)
                if hd == 2 * (KC - 1):
                    mm.then_inc(used, 1)
                nc.tensor.matmul(ps[:, bank, P:3 * P], q[o:o + HD, t, P:2 * P], kd[o:o + HD, g, :], start=True, stop=True).then_inc(scores, 1)

            def turn_probs(hd):
                pe.wait_ge(norm_done, hd + 1)
                if hd >= 2:
                    pe.wait_ge(p_copied, hd - 1)
                for m in range(3):
                    mm = nc.tensor.transpose(ps[:, 4 + hd % 2, m * P:(m + 1) * P], probs[:, hd % 3, m * P:(m + 1) * P], ident)
                mm.then_inc(p_turned, 1)

            def weigh_values(hd):
                pe.wait_ge(p_copied, hd + 1)
                if hd >= 2:
                    pe.wait_ge(heads_ready, hd // 2)
                o, g, pt = (hd % 2) * HD, hd // GROUP, probs_t[:, hd % 2]
                v = [v_tok[:, b, g * HD:(g + 1) * HD] for b in range(TT)]
                nc.tensor.matmul(ps[o:o + HD, 6, 0:P], v[0], pt[:, 0:P], start=True, stop=True)
                nc.tensor.matmul(ps[o:o + HD, 6, P:2 * P], v[0], pt[:, P:2 * P], start=True, stop=False)
                mm = nc.tensor.matmul(ps[o:o + HD, 6, P:2 * P], v[1], pt[:, 2 * P:3 * P], start=False, stop=True)
                if hd % 2:
                    mm.then_inc(heads_ps, 1)

            pe.wait_ge(kd_ready, NKV)
            project_q(0)
            rotate_q(0)
            for t in range(KC + 1):
                if t + 1 < KC:
                    project_q(t + 1)
                if t < KC:
                    score(2 * t)
                    score(2 * t + 1)
                if t >= 1:
                    turn_probs(2 * t - 2)
                    turn_probs(2 * t - 1)
                if t + 1 < KC:
                    rotate_q(t + 1)
                if t >= 1:
                    weigh_values(2 * t - 2)
                    weigh_values(2 * t - 1)
            for t in range(KC):
                arrived(FIRST_ATT + 6 + t // 2)
                if t >= 4:
                    pe.wait_ge(h_ready, 3 * KC + t - 3)
                mm = tile(t % 4, as_columns(slot_of[FIRST_ATT + 6 + t // 2]), (t % 2) * P, heads,
                          (lambda k: pe.wait_ge(heads_ready, k + 1)) if t == 0 else None, frees=t in (2, 4, 6))
                mm.then_inc(wo_proj, 1)
                if t >= 1:
                    sum_square(3, t - 1, 7)
            sum_square(3, KC - 1, 7)

            pe.wait_ge(misc_in, 32)
            pe.wait_ge(hn_ready, 4 * KC)
            for b in range(TT):
                for k in range(KC):
                    mm = nc.tensor.matmul(ps[:, 0, b * E:(b + 1) * E], hn[:, k, b * P:(b + 1) * P], wr[:, k, :], start=(k == 0), stop=(k == KC - 1))
                    if b == 0 and k == 0:
                        mm.then_inc(used, 1)
            mm.then_inc(logits_ready, 1)
            for g in range(4):
                for m in range(4):
                    c = 4 * (g % 2) + m
                    mm = nc.tensor.transpose(ps[:, 2 + g, m * P:(m + 1) * P], hn[:, c, (g // 2) * P:(g // 2 + 1) * P], ident)
                    if (g, m) == (0, 0):
                        mm.then_inc(parts_used, PARTS)
                mm.then_inc(hn_turned, 1)
            pe.wait_ge(sel_ready, 1)
            nc.tensor.matmul(ps[:, 1, 0:E], const("before"), chosen[:, 0], start=True, stop=True)
            nc.tensor.matmul(ps[:, 1, E:2 * E], const("before"), chosen[:, 1], start=True, stop=False)
            nc.tensor.matmul(ps[:, 1, E:2 * E], const("ones"), chosen[:, 0], start=False, stop=True)
            nc.tensor.matmul(ps[:, 1, 2 * E:3 * E], const("ones"), chosen[:, 0], start=True, stop=False)
            nc.tensor.matmul(ps[:, 1, 2 * E:3 * E], const("ones"), chosen[:, 1], start=False, stop=True).then_inc(pos_ready, 1)

            SCATTER_BANK = (5, 4, 5, 4)
            PASSES = ((0, 0), (0, 1), (1, 0))

            def weights_back(i):
                pe.wait_ge(weighted_ready, 2 * i + 2)
                for b in range(TT):
                    mm = nc.tensor.transpose(ps[0:CAP, 4, b * P:(b + 1) * P], selw[:, b], ident)
                mm.then_inc(g_turned, 1)

            def scatter(i, m):
                if m == 0:
                    pe.wait_ge(g_ready, i + 1)
                    pe.wait_ge(y_staged, 2 * i + 1)
                if m >= 2:
                    pe.wait_ge(added, 4 * i + (m - 1))
                for d in (2 * m, 2 * m + 1):
                    mm = nc.tensor.matmul(ps[:, SCATTER_BANK[m], (d % 2) * T:(d % 2 + 1) * T], y_tok[:, d * P:(d + 1) * P], gt, start=True, stop=True)
                mm.then_inc(scattered, 1)

            def item(i):
                def parts(piece):
                    n = MOE_AT[piece]
                    pe.wait_ge(hi_done, PIECES * i + (n + 1))
                    pe.wait_ge(lo_done, PIECES * i + (SLOTS + n + 1))
                    return w_hi[:, n % PARTS], w_lo[:, n % PARTS]

                pe.wait_ge(onehot_ready, 2 * i + 2)
                for g in range(2):
                    for m in range(4):
                        c = 4 * g + m
                        for b in range(TT):
                            mm = nc.tensor.matmul(ps[:, 4 + g, m * CAP:(m + 1) * CAP], hn_tok[:, b, c * P:(c + 1) * P], sel[:, b],
                                                  start=(b == 0), stop=(b == TT - 1))
                    mm.then_inc(gathered, 1)
                for c in range(NCH + 2):
                    if c < NCH:
                        for m, what in enumerate(("gate", "up")):
                            w = [a.rearrange("p (k c) -> p k c", k=KC) for a in parts((what, c))]
                            if c == 0 and m == 0:
                                pe.wait_ge(xg_ready, 2 * i + 2)
                            xs = (xg_hi, xg_lo)
                            for k in range(KC):
                                for a, b in PASSES:
                                    mm = nc.tensor.matmul(ps[0:CAP, c % 2, m * CHF:(m + 1) * CHF], xs[a][:, k], w[b][:, k],
                                                          start=(k == 0 and (a, b) == (0, 0)), stop=(k == KC - 1 and a == 1))
                            mm.then_inc(parts_used, 1)
                    if c == 0:
                        weights_back(i)
                    if 1 <= c <= NCH:
                        pe.wait_ge(m_h, NCH * i + c)
                        for f in range(2):
                            mm = nc.tensor.transpose(ps[:, 7 - c % 2, f * CAP:(f + 1) * CAP], h_tok[:, (c - 1) % 2, f * P:(f + 1) * P],
                                                     cst[0:CAP, 0:CAP])
                        mm.then_inc(h_turned, 1)
                    if c >= 2:
                        w = [a.rearrange("p (f d) -> p f d", f=2) for a in parts(("down", c - 2))]
                        pe.wait_ge(ht_ready, NCH * i + (c - 1))
                        if c == 2:
                            pe.wait_ge(y_staged, 2 * i + 1)
                        hs = (ht_hi, ht_lo)
                        for f in range(2):
                            for a, b in PASSES:
                                for g in range(2):
                                    mm = nc.tensor.matmul(ps[0:CAP, 2 + g, :], hs[a][:, c % 2, f], w[b][:, f, g * 512:(g + 1) * 512],
                                                          start=(c == 2 and f == 0 and (a, b) == (0, 0)),
                                                          stop=(c == NCH + 1 and f == 1 and a == 1))
                        mm.then_inc(parts_used, 1)
                    if c in (3, 5):
                        scatter(i, c - 3)
                        scatter(i, c - 2)

            pe.wait_ge(hn_tok_ready, 4)
            with pe.Fori(0, E) as i:
                item(i)
            pe.wait_ge(table_ready, 1)
            n_over = pe.value_load(table[0:1, 0:1], min_val=0, max_val=MAX_OVER)
            with pe.Fori(0, MAX_OVER) as o:
                with pe.If(o < n_over):
                    item(o + E)
            last = n_over + E
            weights_back(last)
            for m in range(4):
                scatter(last, m)
            for c in range(KC):
                sum_square(4, c, 0)

            pe.wait_ge(hn_ready, 5 * KC)
            for g in range(8):
                for m in range(2):
                    c = 2 * (g % 4) + m
                    mm = nc.tensor.transpose(ps[:, g, m * P:(m + 1) * P], hn[:, c, (g // 4) * P:(g // 4 + 1) * P], ident)
                mm.then_inc(out_turned, 1)


_INS = ['x', 'positions', 'norm_mix', 'norm_ffn', 'norm_final', 'lru_w_in', 'lru_conv_w', 'lru_conv_b', 'lru_w_a',
        'lru_b_a', 'lru_w_x', 'lru_b_x', 'lru_lambda', 'lru_w_out', 'attn_w_qkv', 'attn_b_qkv', 'attn_sinks',
        'attn_w_o', 'attn_b_o', 'ffn_w_gate', 'ffn_w_up', 'ffn_w_down', 'moe_w_router', 'moe_w_gate', 'moe_w_up',
        'moe_w_down']


def kernel(**inputs):
    import numpy as _np
    import concourse.bacc as _bacc
    from concourse import mybir as _mybir
    from concourse.bass_utils import run_bass_kernel_spmd as _run

    nc = _bacc.Bacc("TRN2", target_bir_lowering=False, num_devices=1)
    arrays, args = {}, []
    for name in _INS:
        a = _np.ascontiguousarray(inputs[name])
        arrays[f"in_{name}"] = a
        args.append(nc.dram_tensor(f"in_{name}", a.shape, _mybir.dt.from_np(a.dtype), kind="ExternalInput").ap())
    c = constant_table()
    arrays["in_consts"] = c
    args.append(nc.dram_tensor("in_consts", c.shape, _mybir.dt.from_np(c.dtype), kind="ExternalInput").ap())
    args.append(nc.dram_tensor("out_0", (1, T, D), _mybir.dt.from_np(_np.dtype("float32")), kind="ExternalOutput").ap())
    trunk(nc, *args)
    r = _run(nc, [arrays], core_ids=[0])
    return r.results[0]["out_0"]
```
